# Optimizing a Trainium2 kernel written in Bass

```python
import jax, jax.numpy as jnp
from jax import lax
import numpy as np

D_MODEL = 2048
BATCH = 1
SEQ = 256
DEPTH = 1
DEC_BATCH = 8
DEC_SEQ = 16
PAST_LEN = 128

CHUNK = 64
HEAD_DIM = 128
A_HEADS = 8
A_LEFT_CHUNKS = 8
A_WINDOW = A_LEFT_CHUNKS * CHUNK
REL_CLIP = 128
B_HEADS = 8
FOX_QBLOCK = 128
A_WIDTH = A_HEADS * HEAD_DIM
B_WIDTH = B_HEADS * HEAD_DIM
PEER_HEADS = 8
PEER_NKEYS = 128
PEER_EXPERTS = PEER_NKEYS * PEER_NKEYS
PEER_TOPK = 16
PEER_QDIM = 256
PEER_HALF = PEER_QDIM // 2
PEER_TOK_BLOCK = 64
FORGET_BIAS_INIT = 3.0
EPS = 1e-6
IN_SPLITS = (A_WIDTH, A_WIDTH, A_WIDTH, B_WIDTH, B_WIDTH, B_WIDTH, B_HEADS, D_MODEL, D_MODEL)
IN_WIDTH = sum(IN_SPLITS)
ATT_SCALE = HEAD_DIM ** -0.5

kernel_name = "hybrid_stream_chunkband_fox_peer_step"

def rmsnorm(x, g):
    xf = x.astype(jnp.float32)
    y = xf * lax.rsqrt(jnp.mean(xf * xf, axis=-1, keepdims=True) + EPS)
    return (y * g.astype(jnp.float32)).astype(x.dtype)

def in_proj(x, ln1, w_in, b_f, qn_a, kn_a, qn_b, kn_b):
    bsz, t = x.shape[0], x.shape[1]
    p = rmsnorm(x, ln1) @ w_in
    qa, ka, va, qb, kb, vb, f, ga, gb = jnp.split(p, np.cumsum(IN_SPLITS)[:-1].tolist(), axis=-1)
    heads = lambda z, h: z.reshape(bsz, t, h, HEAD_DIM)
    qa = rmsnorm(heads(qa, A_HEADS), qn_a)
    ka = rmsnorm(heads(ka, A_HEADS), kn_a)
    qb = rmsnorm(heads(qb, B_HEADS), qn_b)
    kb = rmsnorm(heads(kb, B_HEADS), kn_b)
    lf = jax.nn.log_sigmoid(f.astype(jnp.float32) + b_f.astype(jnp.float32))
    return (qa, ka, heads(va, A_HEADS), qb, kb, heads(vb, B_HEADS), lf,
            jax.nn.sigmoid(ga), jax.nn.sigmoid(gb))

def band_attention(q, k, v, qpos, kpos, kvalid, rel_table):
    s = jnp.einsum("bnqhd,bnkhd->bhnqk", q, k).astype(jnp.float32) * ATT_SCALE
    rel = jnp.clip(qpos[:, :, None] - kpos[:, None, :], -REL_CLIP, REL_CLIP) + REL_CLIP
    s = s + rel_table.astype(jnp.float32)[:, rel][None]
    s = jnp.where(kvalid[None, None, :, None, :], s, -jnp.inf)
    p = jax.nn.softmax(s, axis=-1).astype(v.dtype)
    return jnp.einsum("bhnqk,bnkhd->bnqhd", p, v)

def chunk_band_prompt(q, k, v, rel_table):
    bsz, s, h, d = q.shape
    nc = s // CHUNK
    kw = A_WINDOW + CHUNK
    idx = jnp.arange(nc)[:, None] * CHUNK + jnp.arange(kw)[None, :]
    kpos = idx - A_WINDOW
    pad = ((0, 0), (A_WINDOW, 0), (0, 0), (0, 0))
    kband = jnp.pad(k, pad)[:, idx]
    vband = jnp.pad(v, pad)[:, idx]
    qc = q.reshape(bsz, nc, CHUNK, h, d)
    qpos = jnp.arange(s).reshape(nc, CHUNK)
    o = band_attention(qc, kband, vband, qpos, kpos, kpos >= 0, rel_table)
    return o.reshape(bsz, s, h, d)

def chunk_band_sample(q, k, v, cache_k, cache_v, rel_table, past_len):
    t = q.shape[1]
    lc = cache_k.shape[1]
    kk = jnp.concatenate([cache_k.astype(k.dtype), k], axis=1)
    vv = jnp.concatenate([cache_v.astype(v.dtype), v], axis=1)
    qpos = (past_len + jnp.arange(t))[None]
    kpos = jnp.concatenate([past_len - lc + jnp.arange(lc), past_len + jnp.arange(t)])[None]
    valid = jnp.ones(kpos.shape, dtype=bool)
    o = band_attention(q[:, None], kk[:, None], vv[:, None], qpos, kpos, valid, rel_table)
    return o[:, 0]

def fox_core(q, cq, qpos, k, v, ck, kpos):
    s = jnp.einsum("bqhd,bkhd->bhqk", q, k).astype(jnp.float32) * ATT_SCALE
    s = s + jnp.transpose(cq, (0, 2, 1))[..., :, None] - jnp.transpose(ck, (0, 2, 1))[..., None, :]
    s = jnp.where((kpos[None, :] <= qpos[:, None])[None, None], s, -jnp.inf)
    p = jax.nn.softmax(s, axis=-1).astype(v.dtype)
    return jnp.einsum("bhqk,bkhd->bqhd", p, v)

def fox_prompt(q, k, v, lf):
    bsz, s, h, d = q.shape
    c = jnp.cumsum(lf, axis=1)
    nb = s // FOX_QBLOCK
    qb = q.reshape(bsz, nb, FOX_QBLOCK, h, d).swapaxes(0, 1)
    cqb = c.reshape(bsz, nb, FOX_QBLOCK, h).swapaxes(0, 1)
    posb = jnp.arange(s).reshape(nb, FOX_QBLOCK)
    kpos = jnp.arange(s)
    out = lax.map(lambda a: fox_core(a[0], a[1], a[2], k, v, c, kpos), (qb, cqb, posb))
    return out.swapaxes(0, 1).reshape(bsz, s, h, d)

def fox_sample(q, k, v, lf, cache_k, cache_v, cache_lf, past_len):
    t = q.shape[1]
    kk = jnp.concatenate([cache_k.astype(k.dtype), k], axis=1)
    vv = jnp.concatenate([cache_v.astype(v.dtype), v], axis=1)
    c = jnp.cumsum(jnp.concatenate([cache_lf.astype(jnp.float32), lf], axis=1), axis=1)
    qpos = past_len + jnp.arange(t)
    kpos = jnp.arange(past_len + t)
    return fox_core(q, c[:, past_len:], qpos, kk, vv, c, kpos)

def peer(x2d, w_pq, sub_keys, peer_u, peer_v):
    n = x2d.shape[0]
    npad = (-n) % PEER_TOK_BLOCK
    xp = jnp.pad(x2d, ((0, npad), (0, 0)))
    m = xp.shape[0]
    q = (xp @ w_pq).reshape(m, PEER_HEADS, 2, PEER_HALF)
    s = jnp.einsum("thpc,pnc->thpn", q, sub_keys).astype(jnp.float32)
    hs, hi = lax.top_k(s, PEER_TOPK)
    cand_s = (hs[:, :, 0, :, None] + hs[:, :, 1, None, :]).reshape(m, PEER_HEADS, PEER_TOPK * PEER_TOPK)
    cand_i = (hi[:, :, 0, :, None] * PEER_NKEYS + hi[:, :, 1, None, :]).reshape(m, PEER_HEADS, PEER_TOPK * PEER_TOPK)
    best_s, pos = lax.top_k(cand_s, PEER_TOPK)
    idx = jnp.take_along_axis(cand_i, pos, axis=-1)
    gate = jax.nn.softmax(best_s, axis=-1).astype(x2d.dtype)
    nb = m // PEER_TOK_BLOCK

    def experts(args):
        xb, ib, gb = args
        a = jnp.einsum("thkd,td->thk", peer_u[ib], xb)
        act = jax.nn.gelu(a, approximate=False) * gb
        return jnp.einsum("thk,thkd->td", act, peer_v[ib])

    out = lax.map(experts, (xp.reshape(nb, PEER_TOK_BLOCK, D_MODEL),
                            idx.reshape(nb, PEER_TOK_BLOCK, PEER_HEADS, PEER_TOPK),
                            gate.reshape(nb, PEER_TOK_BLOCK, PEER_HEADS, PEER_TOPK)))
    return out.reshape(m, D_MODEL)[:n]

def merge_ffn(x, ya, yb, ga, gb, w_br_a, w_br_b, w_out, ln2, w_pq, sub_keys, peer_u, peer_v):
    bsz, t = x.shape[0], x.shape[1]
    m = ga * (ya.reshape(bsz, t, A_WIDTH) @ w_br_a) + gb * (yb.reshape(bsz, t, B_WIDTH) @ w_br_b)
    h = x + m @ w_out
    f = peer(rmsnorm(h, ln2).reshape(bsz * t, D_MODEL), w_pq, sub_keys, peer_u, peer_v)
    return h + f.reshape(bsz, t, D_MODEL)

def setup_inputs(seed: int = 0) -> dict:
    key = jax.random.key(seed)
    ks = jax.random.split(key, 24)
    nrm = lambda k, shape, scale: jax.random.normal(k, shape, jnp.float32) * scale
    la = min(A_WINDOW, PAST_LEN)
    return {
        "x_prompt": nrm(ks[0], (BATCH, SEQ, D_MODEL), 1.0),
        "x_sample": nrm(ks[1], (DEC_BATCH, DEC_SEQ, D_MODEL), 1.0),
        "cache_a_k": nrm(ks[2], (DEPTH, DEC_BATCH, la, A_HEADS, HEAD_DIM), 1.0),
        "cache_a_v": nrm(ks[3], (DEPTH, DEC_BATCH, la, A_HEADS, HEAD_DIM), 1.0),
        "cache_b_k": nrm(ks[4], (DEPTH, DEC_BATCH, PAST_LEN, B_HEADS, HEAD_DIM), 1.0),
        "cache_b_v": nrm(ks[5], (DEPTH, DEC_BATCH, PAST_LEN, B_HEADS, HEAD_DIM), 1.0),
        "cache_b_lf": jax.nn.log_sigmoid(FORGET_BIAS_INIT + nrm(ks[6], (DEPTH, DEC_BATCH, PAST_LEN, B_HEADS), 1.0)),
        "ln1": 1.0 + nrm(ks[7], (DEPTH, D_MODEL), 0.02),
        "w_in": nrm(ks[8], (DEPTH, D_MODEL, IN_WIDTH), D_MODEL ** -0.5),
        "b_f": FORGET_BIAS_INIT + nrm(ks[9], (DEPTH, B_HEADS), 0.5),
        "qn_a": 1.0 + nrm(ks[10], (DEPTH, HEAD_DIM), 0.02),
        "kn_a": 1.0 + nrm(ks[11], (DEPTH, HEAD_DIM), 0.02),
        "qn_b": 1.0 + nrm(ks[12], (DEPTH, HEAD_DIM), 0.02),
        "kn_b": 1.0 + nrm(ks[13], (DEPTH, HEAD_DIM), 0.02),
        "rel_bias": nrm(ks[14], (DEPTH, A_HEADS, 2 * REL_CLIP + 1), 0.1),
        "w_br_a": nrm(ks[15], (DEPTH, A_WIDTH, D_MODEL), A_WIDTH ** -0.5),
        "w_br_b": nrm(ks[16], (DEPTH, B_WIDTH, D_MODEL), B_WIDTH ** -0.5),
        "w_out": nrm(ks[17], (DEPTH, D_MODEL, D_MODEL), D_MODEL ** -0.5),
        "ln2": 1.0 + nrm(ks[18], (DEPTH, D_MODEL), 0.02),
        "w_pq": nrm(ks[19], (DEPTH, D_MODEL, PEER_HEADS * PEER_QDIM), D_MODEL ** -0.5),
        "sub_keys": nrm(ks[20], (DEPTH, 2, PEER_NKEYS, PEER_HALF), PEER_HALF ** -0.5),
        "peer_u": nrm(ks[21], (DEPTH, PEER_EXPERTS, D_MODEL), D_MODEL ** -0.5),
        "peer_v": nrm(ks[22], (DEPTH, PEER_EXPERTS, D_MODEL), PEER_HEADS ** -0.5),
    }

def reference(x_prompt, x_sample, cache_a_k, cache_a_v, cache_b_k, cache_b_v, cache_b_lf,
              ln1, w_in, b_f, qn_a, kn_a, qn_b, kn_b, rel_bias, w_br_a, w_br_b, w_out,
              ln2, w_pq, sub_keys, peer_u, peer_v):
    past_len = cache_b_k.shape[2]
    keep = min(A_WINDOW, x_prompt.shape[1])
    hp, hs = x_prompt, x_sample
    akp, avp, aks, avs, bkp, bvp, blp, bks, bvs, bls = ([] for _ in range(10))
    for l in range(DEPTH):
        qa, ka, va, qb, kb, vb, lf, ga, gb = in_proj(hp, ln1[l], w_in[l], b_f[l], qn_a[l], kn_a[l], qn_b[l], kn_b[l])
        ya = chunk_band_prompt(qa, ka, va, rel_bias[l])
        yb = fox_prompt(qb, kb, vb, lf)
        akp.append(ka[:, -keep:]); avp.append(va[:, -keep:])
        bkp.append(kb); bvp.append(vb); blp.append(lf)
        hp = merge_ffn(hp, ya, yb, ga, gb, w_br_a[l], w_br_b[l], w_out[l], ln2[l], w_pq[l], sub_keys[l], peer_u[l], peer_v[l])
        qa, ka, va, qb, kb, vb, lf, ga, gb = in_proj(hs, ln1[l], w_in[l], b_f[l], qn_a[l], kn_a[l], qn_b[l], kn_b[l])
        ya = chunk_band_sample(qa, ka, va, cache_a_k[l], cache_a_v[l], rel_bias[l], past_len)
        yb = fox_sample(qb, kb, vb, lf, cache_b_k[l], cache_b_v[l], cache_b_lf[l], past_len)
        aks.append(ka); avs.append(va)
        bks.append(kb); bvs.append(vb); bls.append(lf)
        hs = merge_ffn(hs, ya, yb, ga, gb, w_br_a[l], w_br_b[l], w_out[l], ln2[l], w_pq[l], sub_keys[l], peer_u[l], peer_v[l])
    return (hp, hs,
            jnp.stack(akp), jnp.stack(avp), jnp.stack(aks), jnp.stack(avs),
            jnp.stack(bkp), jnp.stack(bvp), jnp.stack(blp),
            jnp.stack(bks), jnp.stack(bvs), jnp.stack(bls))


_drawn_inputs = setup_inputs


def setup_inputs(seed=0):
    import zlib

    import numpy as np

    out = dict(_drawn_inputs(seed))
    spreads = {}
    factors = {'ln1': 2.809, 'qn_a': 6.964, 'qn_b': 5.464, 'kn_b': 2.753, 'rel_bias': 3.186, 'ln2': 4.038}
    for name, (base, spread) in spreads.items():
        noise = np.random.default_rng([zlib.crc32(name.encode()), seed]).standard_normal(out[name].shape)
        drawn = base * np.exp(spread * noise) if base else spread * noise
        out[name] = __import__('jax').numpy.asarray(drawn.astype(out[name].dtype))
    for name, factor in factors.items():
        out[name] = (out[name] * factor).astype(out[name].dtype)
    return out
```

```python
from contextlib import ExitStack, contextmanager

import concourse.bass as bass
from concourse import mybir

F32 = mybir.dt.float32
U32 = mybir.dt.uint32
ALU = mybir.AluOpType
ACT = mybir.ActivationFunctionType
AX = mybir.AxisListType.X

P = 128
D = 2048
KT = D // P
TT = 3
T = TT * P
CW = 512
HC = CW // P
NCH = D // CW
KP = 4
NP = KT // KP
HEADS = 8
GROUPS = HEADS // HC
WIDTH = HEADS * P
STREAMS = 8
SQ = P // STREAMS
CHUNK = 64
TOPK = 16
PH = 8
SLOTS = PH * TOPK
BODY = 8
UR = 4
VR = 8
CONSTS = 15
EPS = 1e-6
ATT_SCALE = float(P) ** -0.5
MASKED = -1e30
FCOL = 6 * WIDTH
GCOL = FCOL + HEADS


class Count:

    def __init__(self, sem):
        self.sem, self.at, self.turns = sem, 0, 0

    def inc(self, ins, by=1):
        ins.then_inc(self.sem, by)
        self.at += by

    @property
    def value(self):
        return self.turns + self.at

    @contextmanager
    def over(self, i, n, per):
        before, outer = self.at, self.turns
        self.turns = outer + i * per
        yield
        assert self.at - before == per, (self.at - before, per)
        self.at, self.turns = before + n * per, outer


def build(nc, a):
    ctx = ExitStack()
    with ctx:
        def sb(name, shape, dt=F32):
            return ctx.enter_context(nc.sbuf_tensor(name, shape, dt))

        def sem(name):
            return ctx.enter_context(nc.semaphore(name))

        xT = sb("xT", [P, KT, T])
        wring = sb("wring", [P, NP, KP, CW])
        hx = sb("hx", [P, TT, D])
        yT = sb("yT", [P, 2, HEADS, T])
        share = sb("share", [P, 12288])
        stage = sb("stage", [P, TT, CW])
        normed = sb("normed", [P, TT, CW])

        hflat = hx[:, :, :].rearrange("p t d -> p (t d)")
        qT = hflat[:, 0:HC * T].rearrange("p (j n) -> p j n", j=HC)
        kT = hflat[:, HC * T:2 * HC * T].rearrange("p (j n) -> p j n", j=HC)
        v = hflat[:, 2 * HC * T:2 * HC * T + TT * CW].rearrange("p (t c) -> p t c", t=TT)
        o = 2 * HC * T + TT * CW
        lfb = hflat[:, o:o + TT * HC * P].rearrange("p (t j n) -> p t j n", t=TT, j=HC)

        ckT = share[:, 0:4096].rearrange("p (j b n) -> p j b n", j=HC, b=STREAMS)
        cv = share[:, 4096:8192].rearrange("p (j b n) -> p j b n", j=HC, b=STREAMS)
        biasA = share[:, 8192:12288].rearrange("p (w h n) -> p w h n", w=4, h=HEADS)
        mT = share[:, 0:KT * T].rearrange("p (k n) -> p k n", k=KT)
        gate = share[:, KT * T:KT * T + 2 * TT * CW].rearrange("p (s t c) -> p s t c", s=2, t=TT)
        mix = share[:, KT * T + 2 * TT * CW:KT * T + 4 * TT * CW].rearrange("p (s t c) -> p s t c", s=2, t=TT)
        xn2 = share[:, 0:TT * D].rearrange("p (t d) -> p t d", t=TT)
        ln2b = share[:, TT * D:TT * D + D]
        pqT = share[:, TT * D + D:TT * D + D + HC * T].rearrange("p (j n) -> p j n", j=HC)
        pkeys = yT[:, :, :, :].rearrange("p s h n -> p (s h n)").rearrange("p (t b n) -> p t b n", t=TT, b=2 * PH)
        wflat = wring[:, :, :, :].rearrange("p a b c -> p (a b c)")
        xTflat = xT[:, :, :].rearrange("p k n -> p (k n)")
        yflat = yT[:, :, :, :].rearrange("p s h n -> p (s h n)")
        urow = [wflat[:, D * n:D * n + D] for n in range(UR)]
        vrow = [xTflat[:, D * n:D * n + D] for n in range(3)] + [yflat[:, D * n:D * n + D] for n in range(3)] \
            + [share[:, TT * D + D * n:TT * D + D * n + D] for n in range(2)]

        kval = share[:, 9728:9984].rearrange("p (b k) -> p b k", k=TOPK)
        kidf = share[:, 9984:10240].rearrange("p (b k) -> p b k", k=TOPK)
        kidx = share[:, 10240:10496].bitcast(U32).rearrange("p (b k) -> p b k", k=TOPK)
        cidx = share[:, 10496:10624].bitcast(U32).rearrange("p (h k) -> p h k", k=TOPK)
        cij = share[:, 10624:10880].bitcast(U32).rearrange("p (s k) -> p s k", s=2)
        cijf = share[:, 10880:11136].rearrange("p (s k) -> p s k", s=2)
        bmax = share[:, 11136:11144]
        bsum = share[:, 11144:11152]
        cand = xTflat[:, 0:2048].rearrange("p (h n) -> p h n", h=PH)
        onehot = xTflat[:, 2048:4096].rearrange("p (s k) -> p s k", k=TOPK)

        prob = sb("prob", [P, 2, 5 * P])
        probT = sb("probT", [P, 2, 5 * P])
        cst = sb("cst", [P, 2, P])
        clfb = sb("clfb", [P, HC, STREAMS, SQ])
        nmax = sb("nmax", [P, 2, TT])
        psum_ = sb("rowsum", [P, 2, TT])
        rinv = sb("rinv", [P, 2, TT])
        ident = sb("ident", [P, P])
        tri = sb("tri", [P, P])
        ntri = sb("ntri", [P, P])
        stri = sb("stri", [P, P])
        triB = sb("triB", [P, P])
        ntriB = sb("ntriB", [P, P])
        maskC = sb("maskC", [P, P])
        maskO = sb("maskO", [P, P])
        gains = sb("gains", [P, 4, P])
        ln1s = sb("ln1s", [P, KT])
        bfs = sb("bfs", [P, HEADS])
        wf = sb("wf", [P, KT, HEADS])
        lf = sb("lf", [P, TT, HEADS])
        lfw = sb("lfw", [P, 2, TT, HEADS])
        clf = sb("clf", [P, HEADS, STREAMS])
        subT = sb("subT", [P, 2, P])
        ssq = sb("ssq", [P, 2, TT])
        rstd = sb("rstd", [P, 2, TT])
        hss = sb("hss", [P, TT, HC])
        hrs = sb("hrs", [P, TT, HC])
        hnw = sb("hnw", [P, TT, HC])
        iota16 = sb("iota16", [P, TOPK])
        eidx = sb("eidx", [P, TT, SLOTS], U32)
        gates = sb("gates", [P, TT, SLOTS])
        idxnow = sb("idxnow", [P, 2, BODY], U32)
        dots = sb("dots", [P, 2, UR])
        acts = sb("acts", [P, 2, UR])

        ps = ctx.enter_context(nc.psum_tensor("ps", [P, 8, CW], F32))

        w_loaded = [sem(f"w_loaded{s}") for s in range(NP)]
        piece_done = sem("piece_done")
        x_loaded = sem("x_loaded")
        xT_loaded = sem("xT_loaded")
        small_loaded = sem("small_loaded")
        made = sem("made")
        bias_loaded = sem("bias_loaded")
        masks_ready = sem("masks_ready")
        x_squared = sem("x_squared")
        xT_scaled = sem("xT_scaled")
        rstd_ready = sem("rstd_ready")
        f_done = sem("f_done")
        z_ready = sem("z_ready")
        z_abs = sem("z_abs")
        z_ln = sem("z_ln")
        lf_ready = sem("lf_ready")
        proj_read = sem("proj_read")
        head_normed = sem("head_normed")
        turned = sem("turned")
        placed = sem("placed")
        lfb_ready = sem("lfb_ready")
        cache_loaded = [sem("ck_loaded"), sem("cv_loaded")]
        st_done = sem("st_done")
        st_copied = sem("st_copied")
        s_done = sem("s_done")
        biased = sem("biased")
        max_ready = sem("max_ready")
        exp_done = sem("exp_done")
        p_ready = sem("p_ready")
        pt_done = sem("pt_done")
        pt_copied = sem("pt_copied")
        y_done = sem("y_done")
        y_copied = sem("y_copied")
        k_stored = [sem(f"k_stored{t}") for t in range(TT)]
        v_stored = [sem(f"v_stored{t}") for t in range(TT)]
        lf_stored = sem("lf_stored")
        mix_read = sem("mix_read")
        z_each = sem("z_each")
        sp_turn = sem("sp_turn")
        pool_turn = sem("pool_turn")
        ss_ready = sem("ss_ready")
        root_done = sem("root_done")
        mixed = sem("mixed")
        m_turned = sem("m_turned")
        m_placed = sem("m_placed")
        x_again = sem("x_again")
        h_ready = sem("h_ready")
        h_squared = sem("h_squared")
        ln2_loaded = sem("ln2_loaded")
        xn2_ready = sem("xn2_ready")
        n_turned = sem("n_turned")
        n_placed = sem("n_placed")
        pq_read = sem("pq_read")
        pq_turned = sem("pq_turned")
        pq_placed = sem("pq_placed")
        key_done = sem("key_done")
        key_read = sem("key_read")
        picked = sem("picked")
        gate_exp = sem("gate_exp")
        best_ready = sem("best_ready")
        idx_now = sem("idx_now")
        u_loaded = [sem(f"u_loaded{n}") for n in range(UR)]
        v_loaded = [sem(f"v_loaded{n}") for n in range(VR)]
        acts_ready = sem("acts_ready")
        u_free = sem("u_free")
        v_free = sem("v_free")
        gelu_done = sem("gelu_done")
        y_stored = sem("y_stored")
        dve_order = sem("dve_order")

        block = ctx.enter_context(nc.Block())


        def after(n, s=NP - 1):
            return NP * n + s + 1 + NP

        def full(w, col):
            return [(w, KP * s, col) for s in range(NP)]

        @block.sync
        def _(sp):
            sp.dma_start(xT[:, :, :], a["xT"].rearrange("p (k n) -> p k n", k=KT)).then_inc(xT_loaded, 16)

            def chunk(n, pieces):
                for s, (w, k0, col) in enumerate(pieces):
                    sp.wait_ge(piece_done, NP * n + s + 1)
                    if not isinstance(n, int):
                        sp.sem_inc(sp_turn, 1)
                    src = w[k0 * P:(k0 + KP) * P, bass.ds(col, CW)].rearrange("(k p) c -> p k c", p=P)
                    sp.dma_start(wring[:, s, :, :], src).then_inc(w_loaded[s], 16)

            for br in range(2):
                for g in range(GROUPS):
                    for c in range(3):
                        chunk(3 * (GROUPS * br + g) + c, full(a["w_in"], (3 * br + c) * WIDTH + g * CW))
            n = 6 * GROUPS
            with sp.Fori(0, NCH) as i:
                chunk(n + 3 * i, full(a["w_in"], GCOL + i * CW))
                chunk(n + 3 * i + 1, full(a["w_in"], GCOL + D + i * CW))
                chunk(n + 3 * i + 2, [(a["w_br_a"], 0, i * CW), (a["w_br_a"], KP, i * CW),
                                      (a["w_br_b"], 0, i * CW), (a["w_br_b"], KP, i * CW)])
            n += 3 * NCH
            for w in (a["w_out"], a["w_pq"]):
                with sp.Fori(0, NCH) as i:
                    chunk(n + i, full(w, i * CW))
                n += NCH
            for t in range(TT):
                sp.wait_ge(v_free, VR + SLOTS * (t + 1))
                sp.dma_start(a["y"][t * P:(t + 1) * P, :], hx[:, t, :]).then_inc(y_stored, 16)
            sp.wait_ge(y_stored, 16 * TT)

        @block.gpsimd
        def _(pool):
            made_n = Count(made)

            def link(ins):
                made_n.inc(ins)
                pool.wait_ge(made, made_n.value)

            for t in range(TT):
                pool.dma_start(hx[:, t, :], a["x"][t * P:(t + 1) * P, :]).then_inc(x_loaded, 16)
            for dst, src in ((ln1s[:, :], a["ln1"]), (bfs[:, :], a["b_f"].partition_broadcast(P)),
                             (wf[:, :, :], a["w_f"].rearrange("p (k h) -> p k h", k=KT)),
                             (clf[:, :, :], a["clf"].rearrange("p (h b) -> p h b", h=HEADS)),
                             (subT[:, :, :], a["subT"].rearrange("p (s n) -> p s n", s=2)),
                             (gains[:, 0, :], a["qn_a"].partition_broadcast(P)),
                             (gains[:, 1, :], a["kn_a"].partition_broadcast(P)),
                             (gains[:, 2, :], a["qn_b"].partition_broadcast(P)),
                             (gains[:, 3, :], a["kn_b"].partition_broadcast(P))):
                pool.dma_start(dst, src).then_inc(small_loaded, 16)
            for w, rel in enumerate(("relL", "relD", "relC", "relD")):
                pool.dma_start(biasA[:, w, :, :], a[rel].rearrange("p (h n) -> p h n", h=HEADS)).then_inc(bias_loaded, 16)

            link(pool.memset(ident[:, :], 0.0))
            link(pool.affine_select(out=ident[:, :], in_=ident[:, :], compare_op=ALU.not_equal, fill=1.0,
                                    base=0, pattern=[[-1, P]], channel_multiplier=1))
            link(pool.memset(tri[:, :], 1.0))
            link(pool.affine_select(out=tri[:, :], in_=tri[:, :], compare_op=ALU.is_ge, fill=0.0,
                                    base=0, pattern=[[1, P]], channel_multiplier=-1))
            link(pool.memset(stri[:, :], 1.0))
            link(pool.affine_select(out=stri[:, :], in_=stri[:, :], compare_op=ALU.is_gt, fill=0.0,
                                    base=0, pattern=[[-1, P]], channel_multiplier=1))
            link(pool.tensor_copy(triB[:, :], tri[:, :]))
            t3 = triB[:, :].rearrange("p (b n) -> p b n", b=STREAMS)
            link(pool.affine_select(out=t3, in_=t3, compare_op=ALU.is_ge, fill=0.0,
                                    base=0, pattern=[[-SQ, STREAMS], [0, SQ]], channel_multiplier=1))
            link(pool.tensor_scalar_mul(ntri[:, :], tri[:, :], -1.0))
            link(pool.tensor_scalar_mul(ntriB[:, :], triB[:, :], -1.0))
            link(pool.iota(iota16[:, :], pattern=[[1, TOPK]], base=0, channel_multiplier=0,
                           allow_small_or_imprecise_dtypes=True))
            link(pool.memset(maskC[:, :], 0.0))
            link(pool.affine_select(out=maskC[:, :], in_=maskC[:, :], compare_op=ALU.is_ge, fill=MASKED,
                                    base=0, pattern=[[-1, P]], channel_multiplier=1))
            link(pool.tensor_copy(maskO[:, :], maskC[:, :]))
            m3 = maskO[:, :].rearrange("p (b n) -> p b n", b=STREAMS)
            link(pool.affine_select(out=m3, in_=m3, compare_op=ALU.is_gt, fill=MASKED,
                                    base=SQ, pattern=[[SQ, STREAMS], [0, SQ]], channel_multiplier=-1))
            assert made_n.at == CONSTS
            pool.wait_ge(bias_loaded, 64)
            dd = biasA[:, 1, :, CHUNK:P]
            link(pool.affine_select(out=dd, in_=dd, compare_op=ALU.is_ge, fill=MASKED,
                                    base=-CHUNK, pattern=[[0, HEADS], [0, P - CHUNK]], channel_multiplier=1))
            oo = biasA[:, 3, :, :].rearrange("p h (b n) -> p h b n", b=STREAMS)
            link(pool.affine_select(out=oo, in_=oo, compare_op=ALU.is_ge, fill=MASKED,
                                    base=0, pattern=[[0, HEADS], [-SQ, STREAMS], [0, SQ]], channel_multiplier=1))
            pool.affine_select(out=oo, in_=oo, compare_op=ALU.is_gt, fill=MASKED,
                               base=SQ, pattern=[[0, HEADS], [SQ, STREAMS], [0, SQ]],
                               channel_multiplier=-1).then_inc(masks_ready, 1)

            for G in range(2 * GROUPS):
                br, g = G // GROUPS, G % GROUPS
                if G:
                    pool.wait_ge(y_done, HC * G)
                for sm, dst, src in ((cache_loaded[0], ckT, a["ckT_a" if br == 0 else "ckT_b"]),
                                     (cache_loaded[1], cv, a["cv_a" if br == 0 else "cv_b"])):
                    half = HC * STREAMS * P
                    pool.dma_start(dst, src[:, g * half:(g + 1) * half]
                                   .rearrange("p (j b n) -> p j b n", j=HC, b=STREAMS)).then_inc(sm, 16)
                for t in range(TT):
                    pool.wait_ge(head_normed, 6 * G + 3 + t + 1)
                    pool.dma_start(a["k_a" if br == 0 else "k_b"][t * P:(t + 1) * P, g * CW:(g + 1) * CW],
                                   normed[:, t, :]).then_inc(k_stored[t], 16)
                for t in range(TT):
                    pool.wait_ge(proj_read, 9 * G + 6 + t + 1)
                    pool.dma_start(a["v_a" if br == 0 else "v_b"][t * P:(t + 1) * P, g * CW:(g + 1) * CW],
                                   v[:, t, :]).then_inc(v_stored[t], 16)
                if G == 0:
                    pool.wait_ge(lf_ready, 1)
                    pool.dma_start(a["lf"].rearrange("(t p) h -> p t h", p=P), lf[:, :, :]).then_inc(lf_stored, 16)
            pool.wait_ge(y_copied, 2 * HEADS)
            for t in range(TT):
                pool.wait_ge(v_stored[t], 16 * 2 * GROUPS)
            for t in range(TT):
                pool.dma_start(hx[:, t, :], a["x"][t * P:(t + 1) * P, :]).then_inc(x_again, 16)
            pool.wait_ge(mixed, TT * NCH)
            pool.dma_start(ln2b, a["ln2"].partition_broadcast(P)).then_inc(ln2_loaded, 16)

            pool.wait_ge(picked, TT)
            pool.wait_ge(key_read, TT * NCH)
            eflat = eidx[:, :, :].rearrange("p t s -> p (t s)")
            with pool.Fori(0, TT * SLOTS // BODY // 2) as pair:
                for half in range(2):
                    turn = 2 * pair + half
                    pool.wait_ge(v_free, turn * BODY + 1)
                    pool.sem_inc(pool_turn, 1)
                    pool.tensor_copy(idxnow[:, half, :], eflat[:, bass.ds(turn * BODY, BODY)]).then_inc(idx_now, 1)
                    pool.wait_ge(idx_now, turn + 1)
                    for s in range(BODY):
                        pool.wait_ge(u_free, turn * BODY + s + 1)
                        pool.sem_inc(pool_turn, 1)
                        pool.indirect_dma_start(urow[s % UR], None, a["peer_u"][:, :],
                                                bass.IndirectOffsetOnAxis(ap=idxnow[:, half, s:s + 1], axis=0)
                                                ).then_inc(u_loaded[s % UR], 16)
                    for s in range(BODY):
                        pool.wait_ge(v_free, turn * BODY + s + 1)
                        pool.sem_inc(pool_turn, 1)
                        pool.indirect_dma_start(vrow[s], None, a["peer_v"][:, :],
                                                bass.IndirectOffsetOnAxis(ap=idxnow[:, half, s:s + 1], axis=0)
                                                ).then_inc(v_loaded[s], 16)
            for t in range(TT):
                pool.wait_ge(k_stored[t], 16 * 2 * GROUPS)
            pool.wait_ge(lf_stored, 16)

        @block.tensor
        def _(pe):
            pe.sem_inc(piece_done, NP)
            mm = pe.matmul

            def part(n, s, src, k0, bank, kt=KT):
                pe.wait_ge(w_loaded[s], 16 * (n + 1))
                for k in range(KP):
                    for t in range(TT):
                        last = mm(ps[:, bank + t, :], src[:, k0 + k, t * P:(t + 1) * P], wring[:, s, k, :],
                                  start=(k0 + k == 0), stop=(k0 + k == kt - 1))
                last.then_inc(piece_done, 1)

            def chunk(n, src, bank):
                for s in range(NP):
                    part(n, s, src, KP * s, bank)

            def turn_heads(u0, ready, done, read, src):
                for t in range(TT):
                    u = u0 + t
                    pe.wait_ge(ready, u + 1)
                    if not (isinstance(u, int) and u < 2):
                        pe.wait_ge(read, u - 1)
                    for j in range(HC):
                        last = pe.transpose(ps[:, 6 + t % 2 if TT % 2 == 0 else 6 + (u0 + t) % 2, j * P:(j + 1) * P],
                                            src[:, t, j * P:(j + 1) * P], ident[:, :])
                    last.then_inc(done, 1)

            pe.wait_ge(made, CONSTS)
            pe.wait_ge(xT_scaled, 1)
            for t in range(TT):
                for k in range(KT):
                    last = mm(ps[:, 6, t * HEADS:(t + 1) * HEADS], xT[:, k, t * P:(t + 1) * P], wf[:, k, :],
                              start=(k == 0), stop=(k == KT - 1))
            last.then_inc(f_done, 1)

            for G in range(2 * GROUPS):
                br = G // GROUPS
                H0 = HC * G
                if G:
                    pe.wait_ge(biased, H0)
                chunk(3 * G, xT, 0)
                if G:
                    pe.wait_ge(pt_copied, H0)
                chunk(3 * G + 1, xT, 3)
                if G:
                    pe.wait_ge(y_copied, H0)
                else:
                    pe.wait_ge(z_ready, 1)
                turn_heads(6 * G, head_normed, turned, placed, normed)
                pe.wait_ge(proj_read, 9 * G + TT)
                chunk(3 * G + 2, xT, 0)
                turn_heads(6 * G + TT, head_normed, turned, placed, normed)
                pe.wait_ge(placed, 6 * (G + 1))
                pe.wait_ge(proj_read, 9 * (G + 1))
                pe.wait_ge(cache_loaded[0], 16 * (G + 1))
                if br:
                    pe.wait_ge(lfb_ready, G - GROUPS + 1)

                def q_of(j, t):
                    return qT[:, j, t * P:(t + 1) * P]

                def cached_scores(j):
                    H = H0 + j
                    if H:
                        pe.wait_ge(st_copied, H)
                    out = ps[:, 6, 0:P]
                    if br:
                        mm(out, stri[:, :], clfb[:, j, :, :].rearrange("p b n -> p (b n)"), start=True, stop=True)
                    for b in range(STREAMS):
                        last = mm(out[:, b * SQ:(b + 1) * SQ], ckT[:, j, b, :], q_of(j, 2)[:, b * SQ:(b + 1) * SQ],
                                  start=(not br and b == 0), stop=True, skip_group_check=True)
                    last.then_inc(st_done, 1)

                def scores(j):
                    H = H0 + j
                    if H >= 2:
                        pe.wait_ge(biased, H - 1)
                    A, B = ps[:, j % 2, :], ps[:, 2 + j % 2, :]
                    k01 = kT[:, j, 0:2 * P]
                    sk = dict(skip_group_check=True)
                    mm(A[:, 0:P], q_of(j, 0), k01[:, 0:P], start=True, stop=True, **sk)
                    mm(A[:, P:3 * P], q_of(j, 1), k01, start=False, stop=True, **sk)
                    if br:
                        f0, f1, f2 = (lfb[:, t, j, :] for t in range(TT))
                        for dst, rows, cols in ((A[:, 0:P], f0, ntri), (A[:, 0:P], tri, f0),
                                                (A[:, P:2 * P], f0, stri), (A[:, P:2 * P], tri, f1),
                                                (A[:, 2 * P:3 * P], f1, ntri), (A[:, 2 * P:3 * P], tri, f1)):
                            mm(dst, rows[:, :], cols[:, :], start=False, stop=True, **sk)
                    mm(B[:, P:2 * P], q_of(j, 2), kT[:, j, 2 * P:T], start=True, stop=True, **sk)
                    if br:
                        for dst, rows, cols in ((B[:, P:2 * P], f2, ntriB), (B[:, P:2 * P], triB, f2),
                                                (B[:, 0:P], triB, f2)):
                            mm(dst, rows[:, :], cols[:, :], start=False, stop=True, **sk)
                    pe.wait_ge(st_copied, H + 1)
                    mm(B[:, 0:P], cst[:, j % 2, :], ident[:, :], start=False, stop=True, **sk).then_inc(s_done, 1)

                def turn_probs(j):
                    H = H0 + j
                    pe.wait_ge(p_ready, H + 1)
                    if H:
                        pe.wait_ge(pt_copied, H)
                    for m in range(5):
                        out = ps[:, 4, m * P:(m + 1) * P] if m < 3 else ps[:, 5, (m - 3) * P:(m - 2) * P]
                        last = pe.transpose(out, prob[:, j % 2, m * P:(m + 1) * P], ident[:, :])
                    last.then_inc(pt_done, 1)

                def values(j):
                    H = H0 + j
                    pe.wait_ge(pt_copied, H + 1)
                    if H:
                        pe.wait_ge(y_copied, H)
                    if j == 0:
                        pe.wait_ge(cache_loaded[1], 16 * (G + 1))
                    Y = ps[:, 7, :]
                    sk = dict(skip_group_check=True)

                    def pt(m):
                        return probT[:, j % 2, m * P:(m + 1) * P]

                    def vh(t):
                        return v[:, t, j * P:(j + 1) * P]
                    mm(Y[:, 0:P], vh(0), pt(0), start=True, stop=True, **sk)
                    mm(Y[:, P:2 * P], vh(0), pt(1), start=False, stop=True, **sk)
                    mm(Y[:, P:2 * P], vh(1), pt(2), start=False, stop=True, **sk)
                    mm(Y[:, 2 * P:3 * P], vh(2), pt(4), start=False, stop=True, **sk)
                    for b in range(STREAMS):
                        last = mm(Y[:, 2 * P + b * SQ:2 * P + (b + 1) * SQ], cv[:, j, b, :],
                                  pt(3)[:, b * SQ:(b + 1) * SQ], start=False, stop=True, **sk)
                    last.then_inc(y_done, 1)

                cached_scores(0)
                scores(0)
                cached_scores(1)
                scores(1)
                for j in range(HC):
                    turn_probs(j)
                    if j + 2 < HC:
                        cached_scores(j + 2)
                    values(j)
                    if j + 2 < HC:
                        scores(j + 2)

            n, p0 = 6 * GROUPS, 6 * GROUPS
            pe.wait_ge(y_copied, 2 * HEADS)
            pe.wait_ge(biased, 2 * HEADS)
            pe.wait_ge(pt_copied, 2 * HEADS)
            with pe.Fori(0, NCH) as i:
                pe.wait_ge(mix_read, 2 * TT * i + TT)
                chunk(n + 3 * i, xT, 0)
                pe.wait_ge(mix_read, 2 * TT * i + 2 * TT)
                chunk(n + 3 * i + 1, xT, 3)
                pe.wait_ge(proj_read, 9 * 2 * GROUPS + 2 * TT * i + TT)
                part(n + 3 * i + 2, 0, yT[:, 0, :, :], 0, 0, HEADS)
                part(n + 3 * i + 2, 1, yT[:, 0, :, :], KP, 0, HEADS)
                pe.wait_ge(proj_read, 9 * 2 * GROUPS + 2 * TT * i + 2 * TT)
                part(n + 3 * i + 2, 2, yT[:, 1, :, :], 0, 3, HEADS)
                part(n + 3 * i + 2, 3, yT[:, 1, :, :], KP, 3, HEADS)
                for t in range(TT):
                    pe.wait_ge(mixed, TT * i + t + 1)
                    pe.wait_ge(m_placed, TT * i + t + (TT if t == 0 else TT - 1))
                    for j in range(HC):
                        last = pe.transpose(ps[:, 6 + t % 2, j * P:(j + 1) * P], stage[:, t, j * P:(j + 1) * P],
                                            ident[:, :])
                    last.then_inc(m_turned, 1)
            n += 3 * NCH
            pe.wait_ge(m_placed, TT * NCH + TT)
            for i in range(NCH):
                if i >= 2:
                    pe.wait_ge(h_ready, TT * (i - 1))
                chunk(n + i, mT, 3 * (i % 2))
            n += NCH
            for t in range(TT):
                pe.wait_ge(xn2_ready, t + 1)
                for q in range(KT // HC):
                    c = t * (KT // HC) + q
                    if c >= 2:
                        pe.wait_ge(n_placed, c - 1)
                    for j in range(HC):
                        last = pe.transpose(ps[:, 6 + c % 2, j * P:(j + 1) * P],
                                            xn2[:, t, (q * HC + j) * P:(q * HC + j + 1) * P], ident[:, :])
                    last.then_inc(n_turned, 1)
            pe.wait_ge(n_placed, TT * KT // HC)
            pe.wait_ge(h_ready, TT * NCH)
            for i in range(NCH):
                if i:
                    pe.wait_ge(pq_read, TT * i)
                chunk(n + i, xT, 0)
                for t in range(TT):
                    u = TT * i + t
                    pe.wait_ge(pq_read, u + 1)
                    if u >= 2:
                        pe.wait_ge(pq_placed, u - 1)
                    for j in range(HC):
                        last = pe.transpose(ps[:, 6 + u % 2, j * P:(j + 1) * P], stage[:, t, j * P:(j + 1) * P],
                                            ident[:, :])
                    last.then_inc(pq_turned, 1)
                for t in range(TT):
                    u = TT * i + t
                    pe.wait_ge(pq_placed, u + 1)
                    if u >= 2:
                        pe.wait_ge(key_read, u - 1)
                    for j in range(HC):
                        last = mm(ps[:, 3 + u % 2, j * P:(j + 1) * P], pqT[:, j, t * P:(t + 1) * P], subT[:, j % 2, :],
                                  start=(j == 0), stop=True, skip_group_check=True)
                    last.then_inc(key_done, 1)

        @block.scalar
        def _(act):
            act.sem_inc(m_placed, TT)
            act.wait_ge(x_loaded, 16 * TT)
            for t in range(TT):
                act.activation(yflat[:, 0:D], hx[:, t, :], ACT.Square, accum_out=ssq[:, 0, t:t + 1]).then_inc(x_squared, 1)
                act.wait_ge(x_squared, t + 1)
            act.wait_ge(ss_ready, 1)
            act.activation(rstd[:, 0, :], rstd[:, 0, :], ACT.Sqrt).then_inc(root_done, 1)
            act.wait_ge(z_ready, 1)
            act.activation(lfw[:, 1, :, :], lfw[:, 0, :, :], ACT.Abs).then_inc(z_abs, 1)
            act.wait_ge(z_abs, 1)
            act.activation(lfw[:, 1, :, :], lfw[:, 1, :, :], ACT.Exp, scale=-1.0).then_inc(z_abs, 1)
            act.wait_ge(z_abs, 2)
            act.activation(lfw[:, 1, :, :], lfw[:, 1, :, :], ACT.Ln, bias=1.0).then_inc(z_ln, 1)
            act.wait_ge(rstd_ready, 1)

            def place(u0, dst):
                for t in range(TT):
                    act.wait_ge(turned, u0 + t + 1)
                    act.activation(dst[:, :, t * P:(t + 1) * P],
                                   ps[:, 6 + (u0 + t) % 2, :].rearrange("p (j n) -> p j n", j=HC),
                                   ACT.Copy).then_inc(placed, 1)

            for G in range(2 * GROUPS):
                H0 = HC * G
                for c in range(2):
                    act.wait_ge(piece_done, after(3 * G + c))
                    for t in range(TT):
                        u = 6 * G + 3 * c + t
                        if u >= TT:
                            act.wait_ge(head_normed, u - TT + 1)
                        act.activation(stage[:, t, :], ps[:, 3 * c + t, :], ACT.Copy,
                                       scale=rstd[:, 0, t:t + 1]).then_inc(proj_read, 1)
                    if c:
                        place(6 * G, qT)
                    act.wait_ge(ss_ready, 2 * G + c + 2)
                    act.activation(hrs[:, :, :], hrs[:, :, :], ACT.Sqrt).then_inc(root_done, 1)
                act.wait_ge(piece_done, after(3 * G + 2))
                for t in range(TT):
                    if G:
                        act.wait_ge(v_stored[t], 16 * G)
                    act.activation(v[:, t, :], ps[:, t, :], ACT.Copy,
                                   scale=rstd[:, 0, t:t + 1]).then_inc(proj_read, 1)
                place(6 * G + TT, kT)

                def copy_cached(j):
                    H = H0 + j
                    act.wait_ge(st_done, H + 1)
                    act.activation(cst[:, j % 2, :], ps[:, 6, 0:P], ACT.Copy).then_inc(st_copied, 1)

                def exps(j):
                    H = H0 + j
                    act.wait_ge(max_ready, H + 1)
                    for t, (c0, c1) in enumerate(((0, P), (P, 3 * P), (3 * P, 5 * P))):
                        last = act.activation(prob[:, j % 2, c0:c1], prob[:, j % 2, c0:c1], ACT.Exp,
                                              bias=nmax[:, j % 2, t:t + 1], accum_out=psum_[:, j % 2, t:t + 1])
                    last.then_inc(exp_done, 1)

                def copy_probs(j):
                    H = H0 + j
                    act.wait_ge(pt_done, H + 1)
                    act.activation(probT[:, j % 2, 0:3 * P], ps[:, 4, 0:3 * P], ACT.Copy)
                    act.activation(probT[:, j % 2, 3 * P:5 * P], ps[:, 5, 0:2 * P], ACT.Copy).then_inc(pt_copied, 1)

                def copy_y(j):
                    H = H0 + j
                    act.wait_ge(y_done, H + 1)
                    act.activation(yT[:, H // HEADS, H % HEADS, :], ps[:, 7, 0:T], ACT.Copy).then_inc(y_copied, 1)

                copy_cached(0)
                copy_cached(1)
                exps(0)
                exps(1)
                for j in range(HC):
                    if j < 2:
                        copy_probs(j)
                        copy_cached(j + 2)
                        copy_y(j)
                        exps(j + 2)
                    else:
                        copy_probs(j)
                        copy_y(j)

            with act.Fori(0, NCH) as i:
                for s in range(2):
                    act.wait_ge(piece_done, after(6 * GROUPS + 3 * i + s))
                    act.wait_ge(mix_read, 2 * TT * i + TT * (s + 1))
                    for t in range(TT):
                        act.activation(gate[:, s, t, :], ps[:, 3 * s + t, :], ACT.Sigmoid,
                                       scale=rstd[:, 0, t:t + 1]).then_inc(proj_read, 1)
                for t in range(TT):
                    act.wait_ge(m_turned, TT * i + t + 1)
                    act.activation(mT[:, bass.ds(i * HC, HC), t * P:(t + 1) * P],
                                   ps[:, 6 + t % 2, :].rearrange("p (j n) -> p j n", j=HC), ACT.Copy
                                   ).then_inc(m_placed, 1)
            act.wait_ge(h_ready, TT * NCH)
            for t in range(TT):
                act.activation(yflat[:, 0:D], hx[:, t, :], ACT.Square, accum_out=ssq[:, 1, t:t + 1]).then_inc(h_squared, 1)
                act.wait_ge(h_squared, t + 1)
            act.wait_ge(ss_ready, 4 * GROUPS + 2)
            act.activation(rstd[:, 1, :], rstd[:, 1, :], ACT.Sqrt).then_inc(root_done, 1)
            for t in range(TT):
                for q in range(KT // HC):
                    c = t * (KT // HC) + q
                    act.wait_ge(n_turned, c + 1)
                    act.activation(xT[:, q * HC:(q + 1) * HC, t * P:(t + 1) * P],
                                   ps[:, 6 + c % 2, :].rearrange("p (j n) -> p j n", j=HC), ACT.Copy
                                   ).then_inc(n_placed, 1)
            for i in range(NCH):
                act.wait_ge(piece_done, after(6 * GROUPS + 4 * NCH + i))
                for t in range(TT):
                    if i:
                        act.wait_ge(pq_turned, TT * (i - 1) + t + 1)
                    act.activation(stage[:, t, :], ps[:, t, :], ACT.Copy).then_inc(pq_read, 1)
                for t in range(TT):
                    act.wait_ge(pq_turned, TT * i + t + 1)
                    if i:
                        act.wait_ge(key_done, TT * i)
                    act.activation(pqT[:, :, t * P:(t + 1) * P],
                                   ps[:, 6 + (TT * i + t) % 2, :].rearrange("p (j n) -> p j n", j=HC), ACT.Copy
                                   ).then_inc(pq_placed, 1)
                for t in range(TT):
                    act.wait_ge(key_done, TT * i + t + 1)
                    act.activation(pkeys[:, t, i * HC:(i + 1) * HC, :],
                                   ps[:, 3 + (TT * i + t) % 2, :].rearrange("p (j n) -> p j n", j=HC), ACT.Copy
                                   ).then_inc(key_read, 1)
            for t in range(TT):
                act.wait_ge(best_ready, t + 1)
                act.activation(gates[:, t, :], gates[:, t, :], ACT.Exp).then_inc(gate_exp, 1)
            with act.Fori(0, TT * SLOTS // BODY) as turn:
                for q in range(BODY // UR):
                    act.wait_ge(u_free, turn * BODY + (q + 1) * UR + UR)
                    act.activation(dots[:, q, :], dots[:, q, :], ACT.Gelu).then_inc(gelu_done, 1)

        @block.vector
        def _(dve):
            order = Count(dve_order)

            def link(ins):
                order.inc(ins)
                dve.wait_ge(dve_order, order.value)

            def step(ins):
                order.inc(ins)

            def settle():
                dve.wait_ge(dve_order, order.value)

            dve.sem_inc(mix_read, 2 * TT)
            dve.sem_inc(u_free, UR)
            dve.sem_inc(v_free, VR)
            dve.wait_ge(small_loaded, 16 * 9)
            dve.wait_ge(xT_loaded, 16)
            for k in range(KT):
                last = dve.tensor_scalar(xT[:, k, :], xT[:, k, :], ln1s[:, k:k + 1], None, ALU.mult)
            last.then_inc(xT_scaled, 1)
            for c in (0, 2):
                link(dve.tensor_scalar(gains[:, c, :], gains[:, c, :], ATT_SCALE, None, ALU.mult))

            roots = Count(root_done)

            def root(dst, src, work, width):
                link(dve.tensor_scalar(src, src, 1.0 / width, EPS, ALU.mult, ALU.add))
                dve.reciprocal(dst, src).then_inc(ss_ready, 1)
                roots.at += 1
                dve.wait_ge(root_done, roots.value)
                link(dve.tensor_tensor(work, dst, dst, ALU.mult))
                link(dve.tensor_tensor(work, work, src, ALU.mult))
                link(dve.tensor_scalar(work, work, -0.5, 1.5, ALU.mult, ALU.add))
                link(dve.tensor_tensor(dst, dst, work, ALU.mult))

            dve.wait_ge(x_squared, TT)
            root(rstd[:, 0, :], ssq[:, 0, :], hnw[:, 0, 0:TT], D)
            dve.sem_inc(rstd_ready, 1)
            dve.wait_ge(f_done, 1)
            for t in range(TT):
                dve.scalar_tensor_tensor(lfw[:, 0, t, :], ps[:, 6, t * HEADS:(t + 1) * HEADS], rstd[:, 0, t:t + 1],
                                         bfs[:, :], ALU.mult, ALU.add).then_inc(z_each, 1)
            dve.wait_ge(z_each, TT)
            dve.sem_inc(z_ready, 1)
            dve.wait_ge(z_ln, 1)
            dve.scalar_tensor_tensor(lf[:, :, :], lfw[:, 0, :, :], 0.0, lfw[:, 1, :, :], ALU.min,
                                     ALU.subtract).then_inc(lf_ready, 1)

            for G in range(2 * GROUPS):
                br, g = G // GROUPS, G % GROUPS
                H0 = HC * G
                for c in range(2):
                    for t in range(TT):
                        dve.wait_ge(proj_read, 9 * G + 3 * c + t + 1)
                        if c:
                            dve.wait_ge(turned, 6 * G + t + 1)
                        elif G:
                            dve.wait_ge(turned, 6 * G - TT + t + 1)
                            dve.wait_ge(k_stored[t], 16 * G)
                        link(dve.tensor_tensor(normed[:, t, :], stage[:, t, :], stage[:, t, :], ALU.mult))
                        link(dve.tensor_reduce(hss[:, t, :], normed[:, t, :].rearrange("p (j n) -> p j n", j=HC), AX,
                                               ALU.add))
                    root(hrs[:, :, :], hss[:, :, :], hnw[:, :, :], P)
                    for t in range(TT):
                        for j in range(HC):
                            blk = slice(j * P, (j + 1) * P)
                            last = dve.scalar_tensor_tensor(normed[:, t, blk], stage[:, t, blk], hrs[:, t, j:j + 1],
                                                            gains[:, 2 * br + c, :], ALU.mult, ALU.mult)
                        last.then_inc(head_normed, 1)
                if br:
                    for j in range(HC):
                        h = HC * g + j
                        dve.wait_ge(lf_ready, 1)
                        for t in range(TT):
                            dve.tensor_copy(lfb[:, t, j, :], lf[:, t, h:h + 1].to_broadcast([P, P]))
                        last = dve.tensor_copy(clfb[:, j, :, :], clf[:, h, :].unsqueeze(2).to_broadcast([P, STREAMS, SQ]))
                    last.then_inc(lfb_ready, 1)
                elif G == 0:
                    dve.wait_ge(masks_ready, 1)

                def bias(j):
                    H, h = H0 + j, HC * g + j
                    dve.wait_ge(s_done, H + 1)
                    if H >= 2:
                        dve.wait_ge(pt_done, H - 1)
                    A, B, X = ps[:, j % 2, :], ps[:, 2 + j % 2, :], prob[:, j % 2, :]
                    if not br:
                        link(dve.tensor_tensor(X[:, 0:P], A[:, 0:P], biasA[:, 1, h, :], ALU.add))
                        link(dve.tensor_tensor(X[:, P:3 * P].rearrange("p (w n) -> p w n", w=2),
                                               A[:, P:3 * P].rearrange("p (w n) -> p w n", w=2),
                                               biasA[:, 0:2, h, :], ALU.add))
                        dve.tensor_tensor(X[:, 3 * P:5 * P].rearrange("p (w n) -> p w n", w=2),
                                          B[:, 0:2 * P].rearrange("p (w n) -> p w n", w=2),
                                          biasA[:, 2:4, h, :], ALU.add).then_inc(biased, 1)
                    else:
                        link(dve.tensor_tensor(X[:, 0:P], A[:, 0:P], maskC[:, :], ALU.add))
                        link(dve.tensor_copy(X[:, P:2 * P], A[:, P:2 * P]))
                        link(dve.tensor_tensor(X[:, 2 * P:3 * P], A[:, 2 * P:3 * P], maskC[:, :], ALU.add))
                        link(dve.tensor_copy(X[:, 3 * P:4 * P], B[:, 0:P]))
                        dve.tensor_tensor(X[:, 4 * P:5 * P], B[:, P:2 * P], maskO[:, :], ALU.add).then_inc(biased, 1)
                    dve.wait_ge(biased, H + 1)
                    for t, (c0, c1) in enumerate(((0, P), (P, 3 * P), (3 * P, 5 * P))):
                        link(dve.tensor_reduce(rinv[:, j % 2, t:t + 1], X[:, c0:c1], AX, ALU.max))
                    dve.tensor_scalar(nmax[:, j % 2, :], rinv[:, j % 2, :], -1.0, None, ALU.mult).then_inc(max_ready, 1)
                    dve.wait_ge(max_ready, H + 1)

                def norm(j):
                    H = H0 + j
                    dve.wait_ge(exp_done, H + 1)
                    X = prob[:, j % 2, :]
                    link(dve.reciprocal(rinv[:, j % 2, :], psum_[:, j % 2, :]))
                    for t, (c0, c1) in enumerate(((0, P), (P, 3 * P), (3 * P, 5 * P))):
                        last = dve.tensor_scalar(X[:, c0:c1], X[:, c0:c1], rinv[:, j % 2, t:t + 1], None, ALU.mult)
                    last.then_inc(p_ready, 1)

                bias(0)
                bias(1)
                norm(0)
                norm(1)
                bias(2)
                norm(2)
                bias(3)
                norm(3)

            with dve.Fori(0, NCH) as i:
                for s in range(2):
                    dve.wait_ge(piece_done, after(6 * GROUPS + 3 * i + 2, 2 * s + 1))
                    for t in range(TT):
                        dve.tensor_tensor(mix[:, s, t, :], ps[:, 3 * s + t, :], gate[:, s, t, :], ALU.mult
                                          ).then_inc(mix_read, 1)
                for t in range(TT):
                    dve.wait_ge(mix_read, 2 * TT * i + 4 * TT)
                    dve.wait_ge(m_placed, TT * i + t + 1)
                    dve.tensor_tensor(stage[:, t, :], mix[:, 0, t, :], mix[:, 1, t, :], ALU.add).then_inc(mixed, 1)
            dve.wait_ge(x_again, 16 * TT)
            for i in range(NCH):
                dve.wait_ge(piece_done, after(6 * GROUPS + 3 * NCH + i))
                for t in range(TT):
                    ht = hx[:, t, i * CW:(i + 1) * CW]
                    dve.tensor_tensor(ht, ps[:, 3 * (i % 2) + t, :], ht, ALU.add).then_inc(h_ready, 1)
            dve.wait_ge(h_squared, TT)
            root(rstd[:, 1, :], ssq[:, 1, :], hnw[:, 0, 0:TT], D)
            dve.wait_ge(ln2_loaded, 16)
            for t in range(TT):
                dve.scalar_tensor_tensor(xn2[:, t, :], hx[:, t, :], rstd[:, 1, t:t + 1], ln2b, ALU.mult,
                                         ALU.mult).then_inc(xn2_ready, 1)

            def top16(value, index, work):
                blocks = range(len(work))
                for half in range(2):
                    lo = 8 * half
                    for b in blocks:
                        step(dve.max(value[b][:, lo:lo + 8], work[b]))
                    settle()
                    for b in blocks:
                        step(dve.max_index(index[b][:, lo:lo + 8], value[b][:, lo:lo + 8], work[b]))
                    settle()
                    if half == 0:
                        for b in blocks:
                            step(dve.match_replace(work[b], value[b][:, 0:8], work[b], -3.0e38))
                        settle()

            dve.wait_ge(key_read, TT * NCH)
            dve.wait_ge(made, CONSTS)
            for t in range(TT):
                top16([kval[:, b, :] for b in range(2 * PH)], [kidx[:, b, :] for b in range(2 * PH)],
                      [pkeys[:, t, b, :] for b in range(2 * PH)])
                for h in range(PH):
                    step(dve.tensor_tensor(cand[:, h, :].rearrange("p (i j) -> p i j", i=TOPK),
                                           kval[:, 2 * h, :].unsqueeze(2).to_broadcast([P, TOPK, TOPK]),
                                           kval[:, 2 * h + 1, :].unsqueeze(1).to_broadcast([P, TOPK, TOPK]), ALU.add))
                settle()
                best = gates[:, t, :].rearrange("p (h k) -> p h k", h=PH)
                top16([best[:, h, :] for h in range(PH)], [cidx[:, h, :] for h in range(PH)],
                      [cand[:, h, :] for h in range(PH)])
                link(dve.tensor_copy(bmax[:, :], best[:, :, 0]))
                dve.tensor_tensor(best, best, bmax[:, :].unsqueeze(2).to_broadcast([P, PH, TOPK]),
                                  ALU.subtract).then_inc(best_ready, 1)
                step(dve.tensor_scalar(cij[:, 0, :], cidx[:, :, :].rearrange("p h k -> p (h k)"), 4, None,
                                       ALU.logical_shift_right))
                step(dve.tensor_scalar(cij[:, 1, :], cidx[:, :, :].rearrange("p h k -> p (h k)"), 15, None,
                                       ALU.bitwise_and))
                step(dve.tensor_copy(kidf[:, :, :], kidx[:, :, :]))
                settle()
                link(dve.tensor_copy(cijf[:, :, :], cij[:, :, :]))
                for half in range(2):
                    link(dve.tensor_tensor(onehot[:, :, :],
                                           cijf[:, half, :].unsqueeze(2).to_broadcast([P, SLOTS, TOPK]),
                                           iota16[:, :].unsqueeze(1).to_broadcast([P, SLOTS, TOPK]), ALU.is_equal))
                    k4 = kidf[:, :, :].rearrange("p (h s) k -> p h s k", s=2)[:, :, half, :]
                    o4 = onehot[:, :, :].rearrange("p (h k) i -> p h k i", h=PH)
                    link(dve.tensor_tensor(o4, o4, k4.unsqueeze(2).to_broadcast([P, PH, TOPK, TOPK]), ALU.mult))
                    link(dve.tensor_reduce(cijf[:, half, :], onehot[:, :, :], AX, ALU.add))
                link(dve.scalar_tensor_tensor(cijf[:, 0, :], cijf[:, 0, :], float(P), cijf[:, 1, :], ALU.mult,
                                              ALU.add))
                link(dve.tensor_copy(eidx[:, t, :], cijf[:, 0, :]))
                dve.wait_ge(gate_exp, t + 1)
                link(dve.tensor_reduce(bsum[:, :], best, AX, ALU.add))
                link(dve.reciprocal(bsum[:, :], bsum[:, :]))
                dve.tensor_tensor(best, best, bsum[:, :].unsqueeze(2).to_broadcast([P, PH, TOPK]),
                                  ALU.mult).then_inc(picked, 1)
            dve.wait_ge(picked, TT)

            TURNS = SLOTS // BODY
            gflat = gates[:, :, :].rearrange("p t s -> p (t s)")
            with dve.Fori(0, TT) as t:
                with dve.Fori(0, TURNS) as i:
                    turn = t * TURNS + i
                    for q in range(BODY // UR):
                        for n in range(UR):
                            dve.wait_ge(u_loaded[n], 16 * (BODY // UR) * turn + 16 * (q + 1))
                            dve.scalar_tensor_tensor(urow[n], urow[n], 1.0, xn2[:, t, :], ALU.mult, ALU.mult,
                                                     accum_out=dots[:, q, n:n + 1]).then_inc(u_free, 1)
                    for q in range(BODY // UR):
                        dve.wait_ge(gelu_done, (BODY // UR) * turn + q + 1)
                        dve.tensor_tensor(acts[:, q, :], dots[:, q, :], gflat[:, bass.ds(turn * BODY + q * UR, UR)],
                                          ALU.mult).then_inc(acts_ready, 1)
                        dve.wait_ge(acts_ready, (BODY // UR) * turn + q + 1)
                        for n in range(UR):
                            s = q * UR + n
                            dve.wait_ge(v_loaded[s], 16 * turn + 16)
                            dve.wait_ge(v_free, VR + turn * BODY + s)
                            dve.scalar_tensor_tensor(hx[:, t, :], vrow[s], acts[:, q, n:n + 1], hx[:, t, :],
                                                     ALU.mult, ALU.add).then_inc(v_free, 1)


def kernel(x_prompt, x_sample, cache_a_k, cache_a_v, cache_b_k, cache_b_v, cache_b_lf, ln1, w_in, b_f,
           qn_a, kn_a, qn_b, kn_b, rel_bias, w_br_a, w_br_b, w_out, ln2, w_pq, sub_keys, peer_u, peer_v):
    import numpy as np
    import concourse.bacc as bacc
    from concourse.bass_utils import run_bass_kernel_spmd

    def tidy(z):
        return np.ascontiguousarray(z)

    x = np.concatenate([np.asarray(x_prompt)[0], np.asarray(x_sample).reshape(P, D)], axis=0)
    w_in0 = np.asarray(w_in)[0]
    table = np.asarray(rel_bias)[0]
    q, k = np.arange(P)[:, None], np.arange(P)[None, :]

    def spread(distance):
        return tidy(table[:, np.clip(distance, -P, P) + P].transpose(1, 0, 2).reshape(P, HEADS * P))

    def keys(c):
        return tidy(np.asarray(c)[0].transpose(3, 2, 0, 1).reshape(P, HEADS * STREAMS * P))

    def values(c):
        return tidy(np.asarray(c)[0].transpose(1, 2, 0, 3).reshape(P, HEADS * STREAMS * P))

    ins = {
        "x": x,
        "xT": tidy(x.T.reshape(KT, P, T).transpose(1, 0, 2).reshape(P, KT * T)),
        "ln1": tidy(np.asarray(ln1)[0].reshape(KT, P).T),
        "ln2": tidy(np.asarray(ln2)[0]),
        "b_f": tidy(np.asarray(b_f)[0]),
        "w_f": tidy(w_in0[:, FCOL:GCOL].reshape(KT, P, HEADS).transpose(1, 0, 2).reshape(P, KT * HEADS)),
        "w_in": w_in0,
        "clf": tidy(np.asarray(cache_b_lf)[0].transpose(1, 2, 0).reshape(P, HEADS * STREAMS)),
        "subT": tidy(np.asarray(sub_keys)[0].transpose(2, 0, 1).reshape(P, 2 * P)),
        "qn_a": np.asarray(qn_a)[0], "kn_a": np.asarray(kn_a)[0],
        "qn_b": np.asarray(qn_b)[0], "kn_b": np.asarray(kn_b)[0],
        "relD": spread(q - k), "relL": spread(P + q - k), "relC": spread(P + q % SQ - k),
        "ckT_a": keys(cache_a_k), "ckT_b": keys(cache_b_k),
        "cv_a": values(cache_a_v), "cv_b": values(cache_b_v),
        "w_br_a": np.asarray(w_br_a)[0], "w_br_b": np.asarray(w_br_b)[0],
        "w_out": np.asarray(w_out)[0], "w_pq": np.asarray(w_pq)[0],
        "peer_u": np.asarray(peer_u)[0], "peer_v": np.asarray(peer_v)[0],
    }
    outs = {"y": (T, D), "k_a": (T, WIDTH), "v_a": (T, WIDTH), "k_b": (T, WIDTH), "v_b": (T, WIDTH), "lf": (T, HEADS)}
    nc = bacc.Bacc("TRN2", target_bir_lowering=False, num_devices=1)
    arrays, aps = {}, {}
    for name, z in ins.items():
        arrays[f"in_{name}"] = np.ascontiguousarray(z)
        aps[name] = nc.dram_tensor(f"in_{name}", z.shape, F32, kind="ExternalInput").ap()
    for name, shape in outs.items():
        aps[name] = nc.dram_tensor(f"out_{name}", shape, F32, kind="ExternalOutput").ap()
    build(nc, aps)
    r = run_bass_kernel_spmd(nc, [arrays], core_ids=[0]).results[0]
    got = {name: np.asarray(r[f"out_{name}"]) for name in outs}
    S = TT * P - P

    def prompt(z, *rest):
        return z[:S].reshape(1, 1, S, *rest)

    def sample(z, *rest):
        return z[S:].reshape(1, STREAMS, SQ, *rest)

    hd = (HEADS, P)
    return (got["y"][:S].reshape(1, S, D), got["y"][S:].reshape(STREAMS, SQ, D),
            prompt(got["k_a"], *hd), prompt(got["v_a"], *hd), sample(got["k_a"], *hd), sample(got["v_a"], *hd),
            prompt(got["k_b"], *hd), prompt(got["v_b"], *hd), prompt(got["lf"], HEADS),
            sample(got["k_b"], *hd), sample(got["v_b"], *hd), sample(got["lf"], HEADS))
```

```python
from contextlib import ExitStack

import concourse.bass as bass
from concourse import mybir

F32 = mybir.dt.float32
U32 = mybir.dt.uint32
ALU = mybir.AluOpType
ACT = mybir.ActivationFunctionType
AX = mybir.AxisListType.X

P = 128
D = 2048
KT = D // P
TT = 3
T = TT * P
CW = 512
HC = CW // P
NCH = D // CW
KP = 4
NP = KT // KP
HEADS = 8
GROUPS = HEADS // HC
WIDTH = HEADS * P
STREAMS = 8
SQ = P // STREAMS
CHUNK = 64
TOPK = 16
PH = 8
SLOTS = PH * TOPK
TURN = 4
TURNS = SLOTS // TURN
IDX = 4
PEELED = 12
NO_TURN = (0, 5)
CONSTS = 15
EPS = 1e-6
ATT_SCALE = float(P) ** -0.5
MASKED = -1e30
FCOL = 6 * WIDTH
GCOL = FCOL + HEADS
CHUNKS = 6 * GROUPS + 5 * NCH
GATES, OUT, PQ = 6 * GROUPS, 6 * GROUPS + 3 * NCH, 6 * GROUPS + 4 * NCH


class Count:

    def __init__(self, sem, by=1):
        self.sem, self.value, self.by = sem, 0, by

    def inc(self, ins):
        ins.then_inc(self.sem, self.by)
        self.value += self.by


class Front:

    def __init__(self, sem, name, tiles, chunk0, streams):
        self.tiles, self.n, self.tokens, self.chunk0, self.streams = tiles, len(tiles), len(tiles) * P, chunk0, streams
        self.blocks = 2 if streams else 3
        self.segments = [(0, 2)] if streams else [(0, 1), (1, 2)]
        self.xT_scaled = sem(f"xT_scaled_{name}")
        self.proj_read = sem(f"proj_read_{name}")
        self.head_normed = sem(f"head_normed_{name}")
        self.turned = sem(f"turned_{name}")
        self.placed = sem(f"placed_{name}")
        self.lfb_ready = sem(f"lfb_ready_{name}")
        self.st_done = sem(f"st_done_{name}")
        self.st_copied = sem(f"st_copied_{name}")
        self.s_done = sem(f"s_done_{name}")
        self.biased = sem(f"biased_{name}")
        self.max_ready = sem(f"max_ready_{name}")
        self.exp_done = sem(f"exp_done_{name}")
        self.p_ready = sem(f"p_ready_{name}")
        self.pt_done = sem(f"pt_done_{name}")
        self.pt_copied = sem(f"pt_copied_{name}")
        self.y_done = sem(f"y_done_{name}")
        self.y_copied = sem(f"y_copied_{name}")
        self.mix_read = sem(f"mix_read_{name}")
        self.prod_ready = sem(f"prod_ready_{name}")
        self.mixed = sem(f"mixed_{name}")
        self.m_turned = sem(f"m_turned_{name}")
        self.m_placed = sem(f"m_placed_{name}")
        self.x_again = sem(f"x_again_{name}")
        self.h_ready = sem(f"h_ready_{name}")
        self.h_squared = sem(f"h_squared_{name}")
        self.ln2_loaded = sem(f"ln2_loaded_{name}")
        self.xn2_ready = sem(f"xn2_ready_{name}")
        self.n_turned = sem(f"n_turned_{name}")
        self.n_placed = sem(f"n_placed_{name}")
        self.pq_read = sem(f"pq_read_{name}")
        self.pq_turned = sem(f"pq_turned_{name}")
        self.pq_placed = sem(f"pq_placed_{name}")
        self.key_done = sem(f"key_done_{name}")
        self.key_read = sem(f"key_read_{name}")
        self.k_stored = sem(f"k_stored_{name}")
        self.v_stored = sem(f"v_stored_{name}")

    def after(self, c, s=NP - 1):
        return NP * (self.chunk0 + c) + s + 1 + NP


class Experts:

    def __init__(self, sem, name, first, turns, urow, vrow):
        self.name, self.first, self.turns, self.urow, self.vrow = name, first, turns, urow, vrow
        self.u_loaded = [sem(f"u_loaded{n}_{name}") for n in range(len(urow))]
        self.v_loaded = [sem(f"v_loaded{n}_{name}") for n in range(len(vrow))]
        self.u_free = sem(f"u_free_{name}")
        self.v_free = sem(f"v_free_{name}")
        self.gelu_done = sem(f"gelu_done_{name}")
        self.acts_ready = sem(f"acts_ready_{name}")
        self.idx_now = sem(f"idx_now_{name}")


def build(nc, a):
    with ExitStack() as ctx:
        def sb(name, shape, dt=F32):
            return ctx.enter_context(nc.sbuf_tensor(name, shape, dt))

        def sem(name):
            return ctx.enter_context(nc.semaphore(name))

        xTr = sb("xTr", [P, KT, 2 * P])
        xTs = sb("xTs", [P, KT, P])
        wring = sb("wring", [P, NP, KP, CW])
        hr = sb("hr", [P, 2 * D])
        hs = sb("hs", [P, D])
        work = sb("work", [P, 3 * D])
        yTr = sb("yTr", [P, 2 * D])
        yTs = sb("yTs", [P, D])
        xn2s = sb("xn2s", [P, D])
        rows = sb("rows", [P, 4, D])
        stage = sb("stage", [P, 2, CW])
        normed = sb("normed", [P, 2, CW])
        pwork = sb("pwork", [P, 12 * P])
        cst = sb("cst", [P, 2, P])
        clfb = sb("clfb", [P, HC, STREAMS, SQ])
        nmax = sb("nmax", [P, 2, 2])
        rowsum = sb("rowsum", [P, 2, 2])
        rinv = sb("rinv", [P, 2, 2])
        ident = sb("ident", [P, P])
        tri = sb("tri", [P, P])
        ntri = sb("ntri", [P, P])
        stri = sb("stri", [P, P])
        triB = sb("triB", [P, P])
        ntriB = sb("ntriB", [P, P])
        maskC = sb("maskC", [P, P])
        maskO = sb("maskO", [P, P])
        gains = sb("gains", [P, 4, P])
        ln1s = sb("ln1s", [P, KT])
        bfs = sb("bfs", [P, HEADS])
        wf = sb("wf", [P, KT, HEADS])
        lf = sb("lf", [P, TT, HEADS])
        lfw = sb("lfw", [P, 2, TT, HEADS])
        clf = sb("clf", [P, HEADS, STREAMS])
        subT = sb("subT", [P, 2, P])
        ssq = sb("ssq", [P, 2, TT])
        rstd = sb("rstd", [P, 2, TT])
        nwork = sb("nwork", [P, TT])
        hss = sb("hss", [P, 2, HC])
        hrs = sb("hrs", [P, 2, HC])
        hnw = sb("hnw", [P, 2, HC])
        iota16 = sb("iota16", [P, TOPK])
        eidx = sb("eidx", [P, TT, SLOTS], U32)
        gates = sb("gates", [P, TT, SLOTS])
        idxnow = {name: sb(f"idxnow_{name}", [P, IDX, TURN], U32) for name in "sr"}
        dots = sb("dots", [P, TURN])
        gelu = sb("gelu", [P, TURN])
        acts = sb("acts", [P, TURN])
        ps = ctx.enter_context(nc.psum_tensor("ps", [P, 8, CW], F32))

        kval = pwork[:, 0:256].rearrange("p (b k) -> p b k", k=TOPK)
        kidf = pwork[:, 256:512].rearrange("p (b k) -> p b k", k=TOPK)
        kidx = pwork[:, 512:768].bitcast(U32).rearrange("p (b k) -> p b k", k=TOPK)
        cidx = pwork[:, 768:896].bitcast(U32).rearrange("p (h k) -> p h k", k=TOPK)
        cij = pwork[:, 896:1152].bitcast(U32).rearrange("p (s k) -> p s k", s=2)
        cijf = pwork[:, 1152:1408].rearrange("p (s k) -> p s k", s=2)
        bmax = pwork[:, 1408:1416]
        bsum = pwork[:, 1416:1424]

        w_loaded = [sem(f"w_loaded{s}") for s in range(NP)]
        piece_done = sem("piece_done")
        x_loaded = sem("x_loaded")
        xTs_loaded = sem("xTs_loaded")
        xTr_loaded = sem("xTr_loaded")
        small_loaded = sem("small_loaded")
        made = sem("made")
        biasS_loaded = sem("biasS_loaded")
        biasR_loaded = sem("biasR_loaded")
        masksS_ready = sem("masksS_ready")
        masksR_ready = sem("masksR_ready")
        x_squared = sem("x_squared")
        rstd_ready = sem("rstd_ready")
        f_done = sem("f_done")
        z_each = sem("z_each")
        z_ready = sem("z_ready")
        z_steps = sem("z_steps")
        lf_ready = sem("lf_ready")
        lf_stored = sem("lf_stored")
        ss_ready = sem("ss_ready")
        root_done = sem("root_done")
        cache_loaded = [sem("ck_loaded"), sem("cv_loaded")]
        best_ready = sem("best_ready")
        gate_exp = sem("gate_exp")
        picked = sem("picked")
        y_stored = sem("y_stored")
        dve_order = sem("dve_order")
        sp_turn = sem("sp_turn")
        pool_turn = sem("pool_turn")

        S = Front(sem, "s", (2,), 0, True)
        R = Front(sem, "r", (0, 1), CHUNKS, False)

        def lay(F, xT, att, y, h, mixed, xn2, prob):
            F.xT, F.h = xT, h
            F.yT = y.rearrange("p (s j n) -> p s j n", s=2, j=HEADS)
            w = HC * F.tokens
            F.qT, F.kT = (att[:, i * w:(i + 1) * w].rearrange("p (j n) -> p j n", j=HC) for i in range(2))
            F.v = att[:, 2 * w:3 * w].rearrange("p (t c) -> p t c", t=F.n)
            F.lfb = att[:, 3 * w:4 * w].rearrange("p (t j n) -> p t j n", t=F.n, j=HC)
            F.mT = mixed[:, 0:KT * F.tokens].rearrange("p (k n) -> p k n", k=KT)
            F.gate = mixed[:, KT * F.tokens:KT * F.tokens + 2 * F.n * CW].rearrange("p (s t c) -> p s t c", s=2, t=F.n)
            F.xn2 = xn2
            F.pkeys = y.rearrange("p (t b n) -> p t b n", t=F.n, b=2 * PH)
            F.pqT = normed[:, 0:F.n, :].rearrange("p t c -> p (t c)").rearrange("p (j n) -> p j n", j=HC)
            F.prob, F.probT = (prob[:, i * 6 * P:i * 6 * P + 2 * F.blocks * P].rearrange("p (w n) -> p w n", w=2)
                               for i in range(2))

        lay(S, xTs, hs[:, :], yTs[:, :], hs[:, :].rearrange("p (t d) -> p t d", t=1), work,
            xn2s[:, :].rearrange("p (t d) -> p t d", t=1), pwork)
        lay(R, xTr, hr[:, :], yTr[:, :], hr[:, :].rearrange("p (t d) -> p t d", t=2), work,
            work[:, 0:2 * D].rearrange("p (t d) -> p t d", t=2), pwork)
        ckT = work[:, 0:2 * D].rearrange("p (j b n) -> p j b n", j=HC, b=STREAMS)
        cv = yTr[:, :].rearrange("p (j b n) -> p j b n", j=HC, b=STREAMS)
        biasS = work[:, 2 * D:3 * D].rearrange("p (w h n) -> p w h n", w=2, h=HEADS)
        biasR = work[:, 0:D].rearrange("p (w h n) -> p w h n", w=2, h=HEADS)
        ln2b = work[:, 2 * D:3 * D]
        S.junk, R.junk = rows[:, 0, :], work[:, 0:D]
        xTs_flat = xTs[:, :, :].rearrange("p k n -> p (k n)")
        xTr_flat = xTr[:, :, :].rearrange("p k n -> p (k n)")
        wflat = wring[:, :, :, :].rearrange("p a b c -> p a (b c)")
        ES = Experts(sem, "s", 2 * SLOTS, TURNS, [rows[:, n, :] for n in (0, 1)],
                     [rows[:, 2, :], rows[:, 3, :], xTs_flat, yTs[:, :]])
        ER = Experts(sem, "r", 0, 2 * TURNS, [wflat[:, n, :] for n in range(NP)], [rows[:, n, :] for n in range(4)])

        block = ctx.enter_context(nc.Block())

        @block.sync
        def _(sp):
            def chunk(n, pieces):
                for s, (w, k0, col) in enumerate(pieces):
                    sp.wait_ge(piece_done, NP * n + s + 1)
                    if not isinstance(n, int):
                        sp.sem_inc(sp_turn, 1)
                    src = w[k0 * P:(k0 + KP) * P, bass.ds(col, CW)].rearrange("(k p) c -> p k c", p=P)
                    sp.dma_start(wring[:, s, :, :], src).then_inc(w_loaded[s], 16)

            def full(w, col):
                return [(w, KP * s, col) for s in range(NP)]

            sp.dma_start(xTs[:, :, :], a["xTs"].rearrange("p (k n) -> p k n", k=KT)).then_inc(xTs_loaded, 16)
            for F in (S, R):
                c0 = F.chunk0
                for G in range(2 * GROUPS):
                    br, g = G // GROUPS, G % GROUPS
                    for c in range(3):
                        chunk(c0 + 3 * G + c, full(a["w_in"], (3 * br + c) * WIDTH + g * CW))
                with sp.Fori(0, NCH) as i:
                    n = i * 3 + (c0 + GATES)
                    chunk(n, full(a["w_in"], GCOL + i * CW))
                    chunk(n + 1, full(a["w_in"], GCOL + D + i * CW))
                    chunk(n + 2, [(a["w_br_a"], 0, i * CW), (a["w_br_a"], KP, i * CW),
                                  (a["w_br_b"], 0, i * CW), (a["w_br_b"], KP, i * CW)])
                sp.wait_ge(F.y_copied, 2 * HEADS)
                sp.wait_ge(F.v_stored, 16 * 2 * GROUPS * F.n)
                sp.dma_start(F.h, a["x"][F.tiles[0] * P:(F.tiles[-1] + 1) * P, :].rearrange("(t p) d -> p t d", p=P)
                             ).then_inc(F.x_again, 16)
                with sp.Fori(0, NCH) as i:
                    chunk(i + (c0 + OUT), full(a["w_out"], i * CW))
                sp.wait_ge(F.mixed, F.n * NCH)
                sp.dma_start(ln2b, a["ln2"].partition_broadcast(P)).then_inc(F.ln2_loaded, 16)
                with sp.Fori(0, NCH) as i:
                    chunk(i + (c0 + PQ), full(a["w_pq"], i * CW))
            sp.wait_ge(ES.v_free, len(ES.vrow) + SLOTS)
            sp.dma_start(a["y"][2 * P:T, :], hs[:, :]).then_inc(y_stored, 16)
            for t in range(2):
                sp.wait_ge(ER.v_free, len(ER.vrow) + SLOTS * (t + 1))
                sp.dma_start(a["y"][t * P:(t + 1) * P, :], R.h[:, t, :]).then_inc(y_stored, 16)
            sp.wait_ge(y_stored, 16 * TT)

        @block.gpsimd
        def _(pool):
            order = Count(made)

            def link(ins):
                order.inc(ins)
                pool.wait_ge(made, order.value)

            def select(m, keep, base, pattern, rows_by, fill):
                return pool.affine_select(out=m, in_=m, compare_op=keep, fill=fill, base=base, pattern=pattern,
                                          channel_multiplier=rows_by)

            for dst, src in ((ln1s[:, :], a["ln1"]), (bfs[:, :], a["b_f"].partition_broadcast(P)),
                             (wf[:, :, :], a["w_f"].rearrange("p (k h) -> p k h", k=KT)),
                             (clf[:, :, :], a["clf"].rearrange("p (h b) -> p h b", h=HEADS)),
                             (subT[:, :, :], a["subT"].rearrange("p (s n) -> p s n", s=2)),
                             (gains[:, 0, :], a["qn_a"].partition_broadcast(P)),
                             (gains[:, 1, :], a["kn_a"].partition_broadcast(P)),
                             (gains[:, 2, :], a["qn_b"].partition_broadcast(P)),
                             (gains[:, 3, :], a["kn_b"].partition_broadcast(P))):
                pool.dma_start(dst, src).then_inc(small_loaded, 16)
            pool.dma_start(S.h, a["x"][2 * P:T, :].rearrange("(t p) d -> p t d", p=P)).then_inc(x_loaded, 16)
            pool.dma_start(R.h, a["x"][0:2 * P, :].rearrange("(t p) d -> p t d", p=P)).then_inc(x_loaded, 16)
            pool.dma_start(xTr[:, :, :], a["xTr"].rearrange("p (k n) -> p k n", k=KT)).then_inc(xTr_loaded, 16)

            link(pool.memset(ident[:, :], 0.0))
            link(select(ident[:, :], ALU.not_equal, 0, [[-1, P]], 1, 1.0))
            link(pool.memset(tri[:, :], 1.0))
            link(select(tri[:, :], ALU.is_ge, 0, [[1, P]], -1, 0.0))
            link(pool.memset(stri[:, :], 1.0))
            link(select(stri[:, :], ALU.is_gt, 0, [[-1, P]], 1, 0.0))
            starts, ends = [[-SQ, STREAMS], [0, SQ]], [[SQ, STREAMS], [0, SQ]]
            link(pool.tensor_copy(triB[:, :], tri[:, :]))
            link(select(triB[:, :].rearrange("p (b n) -> p b n", b=STREAMS), ALU.is_ge, 0, starts, 1, 0.0))
            link(pool.tensor_scalar_mul(ntri[:, :], tri[:, :], -1.0))
            link(pool.tensor_scalar_mul(ntriB[:, :], triB[:, :], -1.0))
            link(pool.iota(iota16[:, :], pattern=[[1, TOPK]], base=0, channel_multiplier=0,
                           allow_small_or_imprecise_dtypes=True))
            link(pool.memset(maskC[:, :], 0.0))
            link(select(maskC[:, :], ALU.is_ge, 0, [[-1, P]], 1, MASKED))
            link(pool.tensor_copy(maskO[:, :], maskC[:, :]))
            link(select(maskO[:, :].rearrange("p (b n) -> p b n", b=STREAMS), ALU.is_gt, SQ, ends, -1, MASKED))
            assert order.value == CONSTS

            for w, rel in enumerate(("relC", "relD")):
                pool.dma_start(biasS[:, w, :, :], a[rel].rearrange("p (h n) -> p h n", h=HEADS)
                               ).then_inc(biasS_loaded, 16)

            def load_caches(G):
                half = HC * STREAMS * P
                lo = (G % GROUPS) * half
                k, w = (("ckT_a", "cv_a"), ("ckT_b", "cv_b"))[G // GROUPS]
                for sm, dst, src in ((cache_loaded[0], ckT, a[k]), (cache_loaded[1], cv, a[w])):
                    pool.dma_start(dst, src[:, lo:lo + half].rearrange("p (j b n) -> p j b n", j=HC, b=STREAMS)
                                   ).then_inc(sm, 16)

            load_caches(0)
            pool.wait_ge(biasS_loaded, 32)
            own = biasS[:, 1, :, :].rearrange("p h (b n) -> p h b n", b=STREAMS)
            link(select(own, ALU.is_ge, 0, [[0, HEADS]] + starts, 1, MASKED))
            select(own, ALU.is_gt, SQ, [[0, HEADS]] + ends, -1, MASKED).then_inc(masksS_ready, 1)

            for G in range(2 * GROUPS):
                if G:
                    pool.wait_ge(S.y_done, HC * G)
                    load_caches(G)
                br, cols = "ab"[G // GROUPS], slice((G % GROUPS) * CW, (G % GROUPS + 1) * CW)
                pool.wait_ge(S.head_normed, 2 * G + 2)
                pool.dma_start(a[f"k_{br}"][2 * P:T, cols], normed[:, 0, :]).then_inc(S.k_stored, 16)
                pool.wait_ge(S.proj_read, 3 * G + 3)
                pool.dma_start(a[f"v_{br}"][2 * P:T, cols], S.v[:, 0, :]).then_inc(S.v_stored, 16)
            pool.wait_ge(lf_ready, 1)
            pool.dma_start(a["lf"].rearrange("(t p) h -> p t h", p=P), lf[:, :, :]).then_inc(lf_stored, 16)

            pool.wait_ge(S.h_ready, NCH)
            for w, rel in enumerate(("relL", "relD")):
                pool.dma_start(biasR[:, w, :, :], a[rel].rearrange("p (h n) -> p h n", h=HEADS)
                               ).then_inc(biasR_loaded, 16)
            pool.wait_ge(biasR_loaded, 32)
            select(biasR[:, 1, :, CHUNK:P], ALU.is_ge, -CHUNK, [[0, HEADS], [0, P - CHUNK]], 1,
                   MASKED).then_inc(masksR_ready, 1)

            eflat = eidx[:, :, :].rearrange("p t s -> p (t s)")

            def gather(E, table, row, loaded, free, count, col):
                pool.wait_ge(free, count)
                pool.sem_inc(pool_turn, 1)
                pool.indirect_dma_start(row, None, table[:, :], bass.IndirectOffsetOnAxis(ap=col, axis=0)
                                        ).then_inc(loaded, 16)

            def turn(E, tau, at, first=False):
                if not first:
                    pool.wait_ge(E.u_free, tau * TURN)
                    pool.sem_inc(pool_turn, 1)
                pool.tensor_copy(idxnow[E.name][:, at, :], eflat[:, bass.ds(tau * TURN + E.first, TURN)]).then_inc(E.idx_now, 1)
                pool.wait_ge(E.idx_now, tau + 1)
                NU, NV = len(E.urow), len(E.vrow)
                for s in range(TURN):
                    gather(E, a["peer_u"], E.urow[s % NU], E.u_loaded[s % NU], E.u_free, tau * TURN + s + 1,
                           idxnow[E.name][:, at, s:s + 1])
                    if not first:
                        gather_v(E, tau - 1, (at - 1) % IDX, s)

            def gather_v(E, tau, at, s):
                NV = len(E.vrow)
                gather(E, a["peer_v"], E.vrow[s % NV], E.v_loaded[s % NV], E.v_free, tau * TURN + s + 1,
                       idxnow[E.name][:, at, s:s + 1])

            for E, ready in ((ES, 1), (ER, 2)):
                pool.wait_ge(picked, ready)
                turn(E, 0, 0, first=True)
                for tau in range(1, IDX):
                    turn(E, tau, tau)

                def body(m):
                    for q in range(IDX):
                        turn(E, m * IDX + q, q)

                if E is ES:
                    with pool.Fori(1, E.turns // IDX) as m:
                        body(m)
                else:
                    with pool.Fori(1, TURNS // IDX) as m:
                        body(m)
                    pool.wait_ge(picked, 3)
                    with pool.Fori(TURNS // IDX, E.turns // IDX) as m:
                        body(m)
                for s in range(TURN):
                    gather_v(E, E.turns - 1, IDX - 1, s)
            pool.wait_ge(S.k_stored, 16 * 2 * GROUPS)
            pool.wait_ge(R.k_stored, 16 * 2 * GROUPS * 2)
            pool.wait_ge(lf_stored, 16)

        @block.tensor
        def _(pe):
            mm = pe.matmul
            sk = dict(skip_group_check=True)
            pe.sem_inc(piece_done, NP)

            def part(F, n, s, src, k0, bank, kt=KT):
                pe.wait_ge(w_loaded[s], (n + 1) * 16)
                for k in range(KP):
                    for t in range(F.n):
                        last = mm(ps[:, bank + t, :], src[:, k0 + k, t * P:(t + 1) * P], wring[:, s, k, :],
                                  start=(k0 + k == 0), stop=(k0 + k == kt - 1))
                last.then_inc(piece_done, 1)

            def chunk(F, n, src, bank):
                for s in range(NP):
                    part(F, n, s, src, KP * s, bank)

            def turn_tiles(F, u0, ready, done, read, src):
                for t in range(F.n):
                    u = u0 + t
                    pe.wait_ge(ready, u + 1)
                    if u >= 2:
                        pe.wait_ge(read, u - 1)
                    for j in range(HC):
                        last = pe.transpose(ps[:, 6 + u % 2, j * P:(j + 1) * P], src(t)[:, j * P:(j + 1) * P],
                                            ident[:, :])
                    last.then_inc(done, 1)

            def group(F, G, prefilled, fill):
                br, H0, n, c0 = G // GROUPS, HC * G, F.n, F.chunk0
                if not prefilled:
                    chunk(F, c0 + 3 * G, F.xT, 0)
                    if F is S and G == 0:
                        forget_gate()
                if G:
                    pe.wait_ge(F.proj_read, 3 * n * (G - 1) + 2 * n)
                chunk(F, c0 + 3 * G + 1, F.xT, 2)
                if G:
                    pe.wait_ge(F.pt_copied, H0)
                    pe.wait_ge(F.y_copied, H0)
                else:
                    pe.wait_ge(z_ready, 1)
                    pe.wait_ge(made, CONSTS)
                turn_tiles(F, 2 * n * G, F.head_normed, F.turned, F.placed, lambda t: normed[:, t, :])
                pe.wait_ge(F.proj_read, 3 * n * G + n)
                chunk(F, c0 + 3 * G + 2, F.xT, 0)
                turn_tiles(F, 2 * n * G + n, F.head_normed, F.turned, F.placed, lambda t: normed[:, t, :])
                pe.wait_ge(F.placed, 2 * n * (G + 1))
                pe.wait_ge(F.proj_read, 3 * n * (G + 1))
                if br:
                    pe.wait_ge(F.lfb_ready, G - GROUPS + 1)
                if F.streams:
                    pe.wait_ge(cache_loaded[0], 16 * (G + 1))

                def q_of(j, t):
                    return F.qT[:, j, t * P:(t + 1) * P]

                def cached_scores(j):
                    if H0 + j:
                        pe.wait_ge(F.st_copied, H0 + j)
                    out = ps[:, 3, 0:P]
                    if br:
                        mm(out, stri[:, :], clfb[:, j, :, :].rearrange("p b n -> p (b n)"), start=True, stop=True)
                    for b in range(STREAMS):
                        last = mm(out[:, b * SQ:(b + 1) * SQ], ckT[:, j, b, :], q_of(j, 0)[:, b * SQ:(b + 1) * SQ],
                                  start=(not br and b == 0), stop=True, **sk)
                    last.then_inc(F.st_done, 1)

                def scores(j):
                    H = H0 + j
                    if H >= 2:
                        pe.wait_ge(F.biased, H - 1)
                    A = ps[:, 4 + j % 2, :]
                    if F.streams:
                        mm(A[:, P:2 * P], q_of(j, 0), F.kT[:, j, :], start=True, stop=True, **sk)
                        f = F.lfb[:, 0, j, :] if br else None
                        extra = ((1, f, ntriB), (1, triB, f), (0, triB, f)) if br else ()
                    else:
                        mm(A[:, 0:P], q_of(j, 0), F.kT[:, j, 0:P], start=True, stop=True, **sk)
                        mm(A[:, P:3 * P], q_of(j, 1), F.kT[:, j, :], start=False, stop=True, **sk)
                        f0, f1 = (F.lfb[:, t, j, :] for t in range(2)) if br else (None, None)
                        extra = ((0, f0, ntri), (0, tri, f0), (1, f0, stri), (1, tri, f1), (2, f1, ntri),
                                 (2, tri, f1)) if br else ()
                    last = None
                    for m, left, right in extra:
                        last = mm(A[:, m * P:(m + 1) * P], left[:, :], right[:, :], start=False, stop=True, **sk)
                    if F.streams:
                        pe.wait_ge(F.st_copied, H + 1)
                        last = mm(A[:, 0:P], cst[:, j % 2, :], ident[:, :], start=False, stop=True, **sk)
                    elif last is None:
                        last = mm(A[:, 3 * P:3 * P + 1], ident[:, :], ident[:, 0:1], start=False, stop=True, **sk)
                    last.then_inc(F.s_done, 1)

                def turn_probs(j):
                    H = H0 + j
                    pe.wait_ge(F.p_ready, H + 1)
                    if H:
                        pe.wait_ge(F.pt_copied, H)
                    for m in range(F.blocks):
                        last = pe.transpose(ps[:, 6, m * P:(m + 1) * P], F.prob[:, j % 2, m * P:(m + 1) * P],
                                            ident[:, :])
                    last.then_inc(F.pt_done, 1)

                def values(j):
                    H = H0 + j
                    pe.wait_ge(F.pt_copied, H + 1)
                    if H:
                        pe.wait_ge(F.y_copied, H)
                    Y = ps[:, 7, :]

                    def pt(m):
                        return F.probT[:, j % 2, m * P:(m + 1) * P]

                    def vh(t):
                        return F.v[:, t, j * P:(j + 1) * P]
                    if F.streams:
                        pe.wait_ge(cache_loaded[1], 16 * (G + 1))
                        mm(Y[:, 0:P], vh(0), pt(1), start=True, stop=True, **sk)
                        for b in range(STREAMS):
                            last = mm(Y[:, b * SQ:(b + 1) * SQ], cv[:, j, b, :], pt(0)[:, b * SQ:(b + 1) * SQ],
                                      start=False, stop=True, **sk)
                    else:
                        mm(Y[:, 0:P], vh(0), pt(0), start=True, stop=True, **sk)
                        mm(Y[:, P:2 * P], vh(0), pt(1), start=False, stop=True, **sk)
                        last = mm(Y[:, P:2 * P], vh(1), pt(2), start=False, stop=True, **sk)
                    last.then_inc(F.y_done, 1)

                def score(j):
                    if F.streams:
                        cached_scores(j)
                    scores(j)

                score(0)
                score(1)
                fill()
                for j in range(HC):
                    turn_probs(j)
                    if j + 2 < HC:
                        if F.streams:
                            cached_scores(j + 2)
                        if j == 0:
                            fill()
                    else:
                        fill()
                    values(j)
                    if j + 2 < HC:
                        scores(j + 2)

            def forget_gate():
                pe.wait_ge(R.xT_scaled, 1)
                for t in range(TT):
                    src = xTr[:, :, t * P:(t + 1) * P] if t < 2 else xTs[:, :, :]
                    for k in range(KT):
                        last = mm(ps[:, 7, t * HEADS:(t + 1) * HEADS], src[:, k, :], wf[:, k, :],
                                  start=(k == 0), stop=(k == KT - 1))
                last.then_inc(f_done, 1)

            def front(F):
                n, c0 = F.n, F.chunk0
                pe.wait_ge(F.xT_scaled, 1)
                filled = 0
                for G in range(2 * GROUPS):
                    pieces = iter(range(NP) if G + 1 < 2 * GROUPS else ())

                    def fill():
                        for s in pieces:
                            part(F, c0 + 3 * (G + 1), s, F.xT, KP * s, 0)
                            break

                    group(F, G, G > 0, fill)

                pe.wait_ge(F.y_copied, 2 * HEADS)
                pe.wait_ge(F.pt_copied, 2 * HEADS)
                with pe.Fori(0, NCH) as i:
                    g0 = c0 + GATES
                    read = 3 * n * 2 * GROUPS
                    pe.wait_ge(F.mix_read, i * (2 * n) + n)
                    chunk(F, i * 3 + g0, F.xT, 0)
                    pe.wait_ge(F.mix_read, i * (2 * n) + 2 * n)
                    chunk(F, i * 3 + (g0 + 1), F.xT, 2)
                    pe.wait_ge(F.proj_read, i * (2 * n) + (read + n))
                    part(F, i * 3 + (g0 + 2), 0, F.yT[:, 0, :, :], 0, 0, HEADS)
                    part(F, i * 3 + (g0 + 2), 1, F.yT[:, 0, :, :], KP, 0, HEADS)
                    pe.wait_ge(F.proj_read, i * (2 * n) + (read + 2 * n))
                    part(F, i * 3 + (g0 + 2), 2, F.yT[:, 1, :, :], 0, 2, HEADS)
                    part(F, i * 3 + (g0 + 2), 3, F.yT[:, 1, :, :], KP, 2, HEADS)
                    for t in range(n):
                        pe.wait_ge(F.mixed, i * n + t + 1)
                        pe.wait_ge(F.m_placed, i * n + t + 1)
                        for j in range(HC):
                            last = pe.transpose(ps[:, 6 + t % 2, j * P:(j + 1) * P], stage[:, t, j * P:(j + 1) * P],
                                                ident[:, :])
                        last.then_inc(F.m_turned, 1)
                pe.wait_ge(F.m_placed, n * NCH + n)
                for i in range(NCH):
                    if i >= 2:
                        pe.wait_ge(F.h_ready, n * (i - 1))
                    chunk(F, c0 + OUT + i, F.mT, 2 * (i % 2))
                for t in range(n):
                    pe.wait_ge(F.xn2_ready, t + 1)
                    for q in range(KT // HC):
                        c = t * (KT // HC) + q
                        if c >= 2:
                            pe.wait_ge(F.n_placed, c - 1)
                        for j in range(HC):
                            last = pe.transpose(ps[:, 6 + c % 2, j * P:(j + 1) * P],
                                                F.xn2[:, t, (q * HC + j) * P:(q * HC + j + 1) * P], ident[:, :])
                        last.then_inc(F.n_turned, 1)
                pe.wait_ge(F.n_placed, n * KT // HC)
                pe.wait_ge(F.h_ready, n * NCH)

                def keys(i):
                    turn_tiles(F, n * i, F.pq_read, F.pq_turned, F.pq_placed, lambda t: stage[:, t, :])
                    for t in range(n):
                        u = n * i + t
                        pe.wait_ge(F.pq_placed, u + 1)
                        if u >= 2:
                            pe.wait_ge(F.key_read, u - 1)
                        for j in range(HC):
                            last = mm(ps[:, 4 + u % 2, j * P:(j + 1) * P], F.pqT[:, j, t * P:(t + 1) * P],
                                      subT[:, j % 2, :], start=(j == 0), stop=True, **sk)
                        last.then_inc(F.key_done, 1)

                for i in range(NCH):
                    if i >= 2:
                        pe.wait_ge(F.pq_read, n * (i - 1))
                    chunk(F, c0 + PQ + i, F.xT, 2 * (i % 2))
                    if i:
                        keys(i - 1)
                keys(NCH - 1)

            front(S)
            front(R)

        @block.scalar
        def _(act):
            roots = [0]

            def root(v):
                roots[0] += 1
                act.wait_ge(ss_ready, roots[0])
                act.activation(v, v, ACT.Sqrt).then_inc(root_done, 1)

            def expert_gelu(E, tau):
                act.wait_ge(E.u_free, tau * TURN + (TURN + len(E.urow)))
                if not (isinstance(tau, int) and tau == 0):
                    act.wait_ge(E.acts_ready, tau)
                act.activation(gelu[:, :], dots[:, :], ACT.Gelu).then_inc(E.gelu_done, 1)

            act.sem_inc(S.m_placed, S.n)
            act.sem_inc(R.m_placed, R.n)
            act.wait_ge(x_loaded, 32)
            for t in range(TT):
                src = R.h[:, t, :] if t < 2 else S.h[:, 0, :]
                act.activation(S.junk, src, ACT.Square, accum_out=ssq[:, 0, t:t + 1]).then_inc(x_squared, 1)
                act.wait_ge(x_squared, t + 1)
            root(rstd[:, 0, :])
            act.wait_ge(rstd_ready, 1)

            def log_sigmoid():
                act.wait_ge(z_ready, 1)
                act.activation(lfw[:, 1, :, :], lfw[:, 0, :, :], ACT.Abs).then_inc(z_steps, 1)
                act.wait_ge(z_steps, 1)
                act.activation(lfw[:, 1, :, :], lfw[:, 1, :, :], ACT.Exp, scale=-1.0).then_inc(z_steps, 1)
                act.wait_ge(z_steps, 2)
                act.activation(lfw[:, 1, :, :], lfw[:, 1, :, :], ACT.Ln, bias=1.0).then_inc(z_steps, 1)

            def front(F, experts):
                n, t0 = F.n, F.tiles[0]

                def blocks(bank):
                    return ps[:, bank, :].rearrange("p (j n) -> p j n", j=HC)

                def place(u0, dst, turned, placed):
                    for t in range(n):
                        act.wait_ge(turned, u0 + t + 1)
                        act.activation(dst[:, :, t * P:(t + 1) * P], blocks(6 + (u0 + t) % 2), ACT.Copy
                                       ).then_inc(placed, 1)

                def scale(t):
                    return rstd[:, 0, t0 + t:t0 + t + 1]

                for G in range(2 * GROUPS):
                    H0, br, cols = HC * G, "ab"[G // GROUPS], slice((G % GROUPS) * CW, (G % GROUPS + 1) * CW)
                    for c in range(2):
                        act.wait_ge(piece_done, F.after(3 * G + c))
                        for t in range(n):
                            u = 2 * n * G + n * c + t
                            if u >= n:
                                act.wait_ge(F.head_normed, u - n + 1)
                            act.activation(stage[:, t, :], ps[:, 2 * c + t, :], ACT.Copy, scale=scale(t)
                                           ).then_inc(F.proj_read, 1)
                        if c:
                            place(2 * n * G, F.qT, F.turned, F.placed)
                        elif F is S and G == 0:
                            log_sigmoid()
                        root(hrs[:, 0:n, :])
                        experts(2 * c + 1 if G or c else 0)
                    act.wait_ge(piece_done, F.after(3 * G + 2))
                    if G:
                        act.wait_ge(F.v_stored, 16 * n * G)
                    for t in range(n):
                        act.activation(F.v[:, t, :], ps[:, t, :], ACT.Copy, scale=scale(t)).then_inc(F.proj_read, 1)
                    place(2 * n * G + n, F.kT, F.turned, F.placed)
                    if not F.streams:
                        act.wait_ge(F.head_normed, 2 * n * (G + 1))
                        act.wait_ge(F.proj_read, 3 * n * (G + 1))
                        for t in range(n):
                            rows_ = slice((t0 + t) * P, (t0 + t + 1) * P)
                            act.dma_start(a[f"k_{br}"][rows_, cols], normed[:, t, :]).then_inc(F.k_stored, 16)
                            act.dma_start(a[f"v_{br}"][rows_, cols], F.v[:, t, :]).then_inc(F.v_stored, 16)

                    def copy_cached(j):
                        if F.streams:
                            act.wait_ge(F.st_done, H0 + j + 1)
                            act.activation(cst[:, j % 2, :], ps[:, 3, 0:P], ACT.Copy).then_inc(F.st_copied, 1)

                    def exps(j):
                        act.wait_ge(F.max_ready, H0 + j + 1)
                        for w, (m, k) in enumerate(F.segments):
                            x = F.prob[:, j % 2, m * P:(m + k) * P]
                            last = act.activation(x, x, ACT.Exp, bias=nmax[:, j % 2, w:w + 1],
                                                  accum_out=rowsum[:, j % 2, w:w + 1])
                        last.then_inc(F.exp_done, 1)

                    def copy_probs(j):
                        act.wait_ge(F.pt_done, H0 + j + 1)
                        act.activation(F.probT[:, j % 2, :], ps[:, 6, 0:F.blocks * P], ACT.Copy
                                       ).then_inc(F.pt_copied, 1)

                    def copy_y(j):
                        H = H0 + j
                        act.wait_ge(F.y_done, H + 1)
                        act.activation(F.yT[:, H // HEADS, H % HEADS, :], ps[:, 7, 0:F.tokens], ACT.Copy
                                       ).then_inc(F.y_copied, 1)

                    copy_cached(0)
                    copy_cached(1)
                    exps(0)
                    exps(1)
                    for j in range(HC):
                        copy_probs(j)
                        if j + 2 < HC:
                            copy_cached(j + 2)
                        copy_y(j)
                        if j + 2 < HC:
                            exps(j + 2)
                    experts(5)

                with act.Fori(0, NCH) as i:
                    for s in range(2):
                        act.wait_ge(piece_done, i * (3 * NP) + F.after(GATES + s))
                        act.wait_ge(F.mix_read, i * (2 * n) + n * (s + 1))
                        for t in range(n):
                            act.activation(F.gate[:, s, t, :], ps[:, 2 * s + t, :], ACT.Sigmoid, scale=scale(t)
                                           ).then_inc(F.proj_read, 1)
                        experts(6, i)
                    for t in range(n):
                        act.wait_ge(F.m_turned, i * n + t + 1)
                        act.activation(F.mT[:, bass.ds(i * HC, HC), t * P:(t + 1) * P], blocks(6 + t % 2), ACT.Copy
                                       ).then_inc(F.m_placed, 1)
                    experts(6, i)
                for i in range(NCH):
                    experts(7)
                act.wait_ge(F.h_ready, n * NCH)
                for t in range(n):
                    act.activation(F.junk, F.h[:, t, :], ACT.Square, accum_out=ssq[:, 1, t0 + t:t0 + t + 1]
                                   ).then_inc(F.h_squared, 1)
                    act.wait_ge(F.h_squared, t + 1)
                root(rstd[:, 1, t0:t0 + n])
                for t in range(n):
                    for q in range(KT // HC):
                        c = t * (KT // HC) + q
                        act.wait_ge(F.n_turned, c + 1)
                        act.activation(F.xT[:, q * HC:(q + 1) * HC, t * P:(t + 1) * P], blocks(6 + c % 2), ACT.Copy
                                       ).then_inc(F.n_placed, 1)
                experts(8)

                def keys(i):
                    for t in range(n):
                        u = n * i + t
                        act.wait_ge(F.pq_turned, u + 1)
                        if i:
                            act.wait_ge(F.key_done, n * i)
                        act.activation(F.pqT[:, :, t * P:(t + 1) * P], blocks(6 + u % 2), ACT.Copy
                                       ).then_inc(F.pq_placed, 1)
                    for t in range(n):
                        u = n * i + t
                        act.wait_ge(F.key_done, u + 1)
                        act.activation(F.pkeys[:, t, i * HC:(i + 1) * HC, :], blocks(4 + u % 2), ACT.Copy
                                       ).then_inc(F.key_read, 1)

                act.wait_ge(F.k_stored, 16 * 2 * GROUPS * n)
                for i in range(NCH):
                    act.wait_ge(piece_done, F.after(PQ + i))
                    for t in range(n):
                        if i:
                            act.wait_ge(F.pq_turned, n * (i - 1) + t + 1)
                        act.activation(stage[:, t, :], ps[:, 2 * (i % 2) + t, :], ACT.Copy).then_inc(F.pq_read, 1)
                    keys(i)
                    experts(9)

            def gate_exps(k):
                t = (2, 0, 1)[k]
                act.wait_ge(best_ready, k + 1)
                act.activation(gates[:, t, :], gates[:, t, :], ACT.Exp).then_inc(gate_exp, 1)

            front(S, lambda *_: None)
            gate_exps(0)

            def s_turns(where, i=None):
                if where in NO_TURN:
                    return
                if i is None:
                    expert_gelu(ES, turns_done[0])
                    turns_done[0] += 1
                else:
                    expert_gelu(ES, i * 3 + (turns_done[0] + in_loop[0]))
                    in_loop[0] += 1
                    if in_loop[0] == 3:
                        in_loop[0] = 0
                        turns_done[0] += 3 * NCH

            turns_done, in_loop = [0], [0]
            front(R, s_turns)
            while turns_done[0] < TURNS:
                expert_gelu(ES, turns_done[0])
                turns_done[0] += 1
                if turns_done[0] == TURNS - 1:
                    gate_exps(1)
            for tau in range(PEELED):
                expert_gelu(ER, tau)
                if tau == PEELED - 4:
                    gate_exps(2)
            with act.Fori(PEELED, 2 * TURNS) as tau:
                expert_gelu(ER, tau)

        @block.vector
        def _(dve):
            order, roots = Count(dve_order), Count(root_done)

            def step(ins):
                order.inc(ins)

            def settle():
                dve.wait_ge(dve_order, order.value)

            def link(ins):
                step(ins)
                settle()

            def root(dst, src, work_, width):
                link(dve.tensor_scalar(src, src, 1.0 / width, EPS, ALU.mult, ALU.add))
                dve.reciprocal(dst, src).then_inc(ss_ready, 1)
                roots.value += 1
                dve.wait_ge(root_done, roots.value)
                link(dve.tensor_tensor(work_, dst, dst, ALU.mult))
                link(dve.tensor_tensor(work_, work_, src, ALU.mult))
                link(dve.tensor_scalar(work_, work_, -0.5, 1.5, ALU.mult, ALU.add))
                link(dve.tensor_tensor(dst, dst, work_, ALU.mult))

            dve.sem_inc(S.mix_read, 2 * S.n)
            dve.sem_inc(R.mix_read, 2 * R.n)
            dve.wait_ge(small_loaded, 16 * 9)
            for F, loaded in ((S, xTs_loaded), (R, xTr_loaded)):
                dve.wait_ge(loaded, 16)
                for k in range(KT):
                    last = dve.tensor_scalar(F.xT[:, k, :], F.xT[:, k, :], ln1s[:, k:k + 1], None, ALU.mult)
                last.then_inc(F.xT_scaled, 1)
            for c in (0, 2):
                link(dve.tensor_scalar(gains[:, c, :], gains[:, c, :], ATT_SCALE, None, ALU.mult))
            dve.wait_ge(x_squared, TT)
            root(rstd[:, 0, :], ssq[:, 0, :], nwork[:, :], D)
            dve.sem_inc(rstd_ready, 1)

            def forget_gate():
                dve.wait_ge(f_done, 1)
                for t in range(TT):
                    dve.scalar_tensor_tensor(lfw[:, 0, t, :], ps[:, 7, t * HEADS:(t + 1) * HEADS],
                                             rstd[:, 0, t:t + 1], bfs[:, :], ALU.mult, ALU.add).then_inc(z_each, 1)
                dve.wait_ge(z_each, TT)
                dve.sem_inc(z_ready, 1)
                dve.wait_ge(z_steps, 3)
                dve.scalar_tensor_tensor(lf[:, :, :], lfw[:, 0, :, :], 0.0, lfw[:, 1, :, :], ALU.min,
                                         ALU.subtract).then_inc(lf_ready, 1)

            def front(F, experts):
                n, t0 = F.n, F.tiles[0]
                for G in range(2 * GROUPS):
                    br, g, H0 = G // GROUPS, G % GROUPS, HC * G
                    for c in range(2):
                        if F is S and G == 0 and c == 0:
                            forget_gate()
                        for t in range(n):
                            dve.wait_ge(F.proj_read, 3 * n * G + n * c + t + 1)
                            if c:
                                dve.wait_ge(F.turned, 2 * n * G + t + 1)
                            elif G:
                                dve.wait_ge(F.turned, 2 * n * G - n + t + 1)
                                dve.wait_ge(F.k_stored, 16 * n * G)
                            elif F is R:
                                dve.wait_ge(S.key_done, NCH)
                            link(dve.tensor_tensor(normed[:, t, :], stage[:, t, :], stage[:, t, :], ALU.mult))
                            link(dve.tensor_reduce(hss[:, t, :], normed[:, t, :].rearrange("p (j n) -> p j n", j=HC),
                                                   AX, ALU.add))
                        root(hrs[:, 0:n, :], hss[:, 0:n, :], hnw[:, 0:n, :], P)
                        for t in range(n):
                            for j in range(HC):
                                blk = slice(j * P, (j + 1) * P)
                                last = dve.scalar_tensor_tensor(normed[:, t, blk], stage[:, t, blk],
                                                                hrs[:, t, j:j + 1], gains[:, 2 * br + c, :],
                                                                ALU.mult, ALU.mult)
                            last.then_inc(F.head_normed, 1)
                        experts(2 * c + 1 if G or c else 0)
                    if br:
                        dve.wait_ge(lf_ready, 1)
                        for j in range(HC):
                            h = HC * g + j
                            for t in range(n):
                                last = dve.tensor_copy(F.lfb[:, t, j, :],
                                                       lf[:, t0 + t, h:h + 1].to_broadcast([P, P]))
                            if F.streams:
                                last = dve.tensor_copy(clfb[:, j, :, :],
                                                       clf[:, h, :].unsqueeze(2).to_broadcast([P, STREAMS, SQ]))
                        last.then_inc(F.lfb_ready, 1)
                    elif G == 0:
                        dve.wait_ge(masksS_ready if F.streams else masksR_ready, 1)

                    def bias(j):
                        H, h = H0 + j, HC * g + j
                        dve.wait_ge(F.s_done, H + 1)
                        if H >= 2:
                            dve.wait_ge(F.pt_done, H - 1)
                        A, X = ps[:, 4 + j % 2, :], F.prob[:, j % 2, :]

                        def two(x):
                            return x.rearrange("p (w n) -> p w n", w=2)
                        if F.streams and not br:
                            dve.tensor_tensor(two(X), two(A[:, 0:2 * P]), biasS[:, :, h, :], ALU.add
                                              ).then_inc(F.biased, 1)
                        elif not br:
                            step(dve.tensor_tensor(X[:, 0:P], A[:, 0:P], biasR[:, 1, h, :], ALU.add))
                            dve.tensor_tensor(two(X[:, P:3 * P]), two(A[:, P:3 * P]), biasR[:, :, h, :], ALU.add
                                              ).then_inc(F.biased, 1)
                        elif F.streams:
                            step(dve.tensor_copy(X[:, 0:P], A[:, 0:P]))
                            dve.tensor_tensor(X[:, P:2 * P], A[:, P:2 * P], maskO[:, :], ALU.add).then_inc(F.biased, 1)
                        else:
                            step(dve.tensor_tensor(X[:, 0:P], A[:, 0:P], maskC[:, :], ALU.add))
                            step(dve.tensor_copy(X[:, P:2 * P], A[:, P:2 * P]))
                            dve.tensor_tensor(X[:, 2 * P:3 * P], A[:, 2 * P:3 * P], maskC[:, :], ALU.add
                                              ).then_inc(F.biased, 1)
                        dve.wait_ge(F.biased, H + 1)
                        for w, (m, k) in enumerate(F.segments):
                            step(dve.tensor_reduce(rinv[:, j % 2, w:w + 1], X[:, m * P:(m + k) * P], AX, ALU.max))
                        settle()
                        dve.tensor_scalar(nmax[:, j % 2, :n], rinv[:, j % 2, :n], -1.0, None, ALU.mult
                                          ).then_inc(F.max_ready, 1)
                        dve.wait_ge(F.max_ready, H + 1)

                    def norm(j):
                        dve.wait_ge(F.exp_done, H0 + j + 1)
                        X = F.prob[:, j % 2, :]
                        link(dve.reciprocal(rinv[:, j % 2, :n], rowsum[:, j % 2, :n]))
                        for w, (m, k) in enumerate(F.segments):
                            x = X[:, m * P:(m + k) * P]
                            last = dve.tensor_scalar(x, x, rinv[:, j % 2, w:w + 1], None, ALU.mult)
                        last.then_inc(F.p_ready, 1)

                    bias(0)
                    bias(1)
                    norm(0)
                    norm(1)
                    bias(2)
                    norm(2)
                    bias(3)
                    norm(3)
                    experts(5)

                with dve.Fori(0, NCH) as i:
                    experts(6, i)
                    experts(6, i)
                    for s in range(2):
                        dve.wait_ge(piece_done, i * (3 * NP) + F.after(GATES + 2, 2 * s + 1))
                        for t in range(n):
                            dve.tensor_tensor(F.gate[:, s, t, :], ps[:, 2 * s + t, :], F.gate[:, s, t, :], ALU.mult
                                              ).then_inc(F.prod_ready, 1)
                    for t in range(n):
                        dve.wait_ge(F.prod_ready, i * (2 * n) + 2 * n)
                        dve.wait_ge(F.m_placed, i * n + t + 1)
                        dve.tensor_tensor(stage[:, t, :], F.gate[:, 0, t, :], F.gate[:, 1, t, :], ALU.add
                                          ).then_inc(F.mixed, 1)
                    dve.sem_inc(F.mix_read, 2 * n)
                    experts(6, i)
                dve.wait_ge(F.x_again, 16)
                for i in range(NCH):
                    dve.wait_ge(piece_done, F.after(OUT + i))
                    for t in range(n):
                        ht = F.h[:, t, i * CW:(i + 1) * CW]
                        dve.tensor_tensor(ht, ps[:, 2 * (i % 2) + t, :], ht, ALU.add).then_inc(F.h_ready, 1)
                    experts(7)
                dve.wait_ge(F.h_squared, n)
                root(rstd[:, 1, t0:t0 + n], ssq[:, 1, t0:t0 + n], nwork[:, t0:t0 + n], D)
                dve.wait_ge(F.ln2_loaded, 16)
                for t in range(n):
                    dve.scalar_tensor_tensor(F.xn2[:, t, :], F.h[:, t, :], rstd[:, 1, t0 + t:t0 + t + 1], ln2b,
                                             ALU.mult, ALU.mult).then_inc(F.xn2_ready, 1)
                experts(8)
                for i in range(NCH):
                    experts(9)

            def top8(value, index, work_, half):
                both = list(zip(value, index, work_))
                lo = 8 * half
                for v_, _, w in both:
                    step(dve.max(v_[:, lo:lo + 8], w))
                settle()
                for v_, x, w in both:
                    step(dve.max_index(x[:, lo:lo + 8], v_[:, lo:lo + 8], w))
                settle()
                if half == 0:
                    for v_, _, w in both:
                        step(dve.match_replace(w, v_[:, 0:8], w, -3.0e38))
                    settle()

            def pick(F, k, cand_at, onehot_at):
                t = (2, 0, 1)[k]
                cand = cand_at.rearrange("p (h n) -> p h n", h=PH)
                onehot = onehot_at.rearrange("p (s k) -> p s k", k=TOPK)
                best = gates[:, t, :].rearrange("p (h k) -> p h k", h=PH)

                def keys(half, lo, hi):
                    def run():
                        r = range(lo, hi)
                        top8([kval[:, b, :] for b in r], [kidx[:, b, :] for b in r],
                             [F.pkeys[:, t - F.tiles[0], b, :] for b in r], half)
                    return run

                def sums():
                    for h in range(PH):
                        step(dve.tensor_tensor(cand[:, h, :].rearrange("p (i j) -> p i j", i=TOPK),
                                               kval[:, 2 * h, :].unsqueeze(2).to_broadcast([P, TOPK, TOPK]),
                                               kval[:, 2 * h + 1, :].unsqueeze(1).to_broadcast([P, TOPK, TOPK]),
                                               ALU.add))
                    settle()

                def bests(half):
                    def run():
                        r = range(PH)
                        top8([best[:, h, :] for h in r], [cidx[:, h, :] for h in r], [cand[:, h, :] for h in r], half)
                    return run

                def places():
                    link(dve.tensor_copy(bmax[:, :], best[:, :, 0]))
                    dve.tensor_tensor(best, best, bmax[:, :].unsqueeze(2).to_broadcast([P, PH, TOPK]),
                                      ALU.subtract).then_inc(best_ready, 1)
                    flat = cidx[:, :, :].rearrange("p h k -> p (h k)")
                    step(dve.tensor_scalar(cij[:, 0, :], flat, 4, None, ALU.logical_shift_right))
                    step(dve.tensor_scalar(cij[:, 1, :], flat, 15, None, ALU.bitwise_and))
                    step(dve.tensor_copy(kidf[:, :, :], kidx[:, :, :]))
                    settle()
                    link(dve.tensor_copy(cijf[:, :, :], cij[:, :, :]))

                def lookup(half):
                    def run():
                        link(dve.tensor_tensor(onehot, cijf[:, half, :].unsqueeze(2).to_broadcast([P, SLOTS, TOPK]),
                                               iota16[:, :].unsqueeze(1).to_broadcast([P, SLOTS, TOPK]),
                                               ALU.is_equal))
                        k4 = kidf[:, :, :].rearrange("p (h s) k -> p h s k", s=2)[:, :, half, :]
                        o4 = onehot.rearrange("p (h k) i -> p h k i", h=PH)
                        link(dve.tensor_tensor(o4, o4, k4.unsqueeze(2).to_broadcast([P, PH, TOPK, TOPK]), ALU.mult))
                        link(dve.tensor_reduce(cijf[:, half, :], onehot, AX, ALU.add))
                    return run

                def finish():
                    link(dve.scalar_tensor_tensor(cijf[:, 0, :], cijf[:, 0, :], float(P), cijf[:, 1, :], ALU.mult,
                                                  ALU.add))
                    link(dve.tensor_copy(eidx[:, t, :], cijf[:, 0, :]))
                    dve.wait_ge(gate_exp, k + 1)
                    link(dve.tensor_reduce(bsum[:, :], best, AX, ALU.add))
                    link(dve.reciprocal(bsum[:, :], bsum[:, :]))
                    dve.tensor_tensor(best, best, bsum[:, :].unsqueeze(2).to_broadcast([P, PH, TOPK]),
                                      ALU.mult).then_inc(picked, 1)
                    dve.wait_ge(picked, k + 1)

                q = 2 * PH // 2
                return [keys(0, 0, q), keys(0, q, 2 * q), keys(1, 0, q), keys(1, q, 2 * q), sums, bests(0), bests(1),
                        places, lookup(0), lookup(1), finish]

            gflat = gates[:, :, :].rearrange("p t s -> p (t s)")

            def expert_acts(E, tau):
                dve.wait_ge(E.gelu_done, tau)
                dve.wait_ge(E.v_free, tau * TURN + (len(E.vrow) - TURN))
                dve.tensor_tensor(acts[:, :], gelu[:, :], gflat[:, bass.ds(tau * TURN + (E.first - TURN), TURN)],
                                  ALU.mult).then_inc(E.acts_ready, 1)
                dve.wait_ge(E.acts_ready, tau)

            def add_row(E, tau, s, h):
                NV = len(E.vrow)
                dve.wait_ge(E.v_loaded[s], tau * 16)
                dve.wait_ge(E.v_free, tau * TURN + (s - TURN + NV))
                dve.scalar_tensor_tensor(h, E.vrow[s], acts[:, s:s + 1], h, ALU.mult, ALU.add).then_inc(E.v_free, 1)

            def expert_turn(E, tau, xn, h, first=False):
                NU = len(E.urow)
                if not first:
                    expert_acts(E, tau)
                for s in range(TURN):
                    u, per = s % NU, TURN // NU
                    dve.wait_ge(E.u_loaded[u], tau * (16 * per) + 16 * (s // NU + 1))
                    dve.scalar_tensor_tensor(E.urow[u], E.urow[u], 1.0, xn, ALU.mult, ALU.mult,
                                             accum_out=dots[:, s:s + 1]).then_inc(E.u_free, 1)
                    if not first:
                        add_row(E, tau, s, h)

            def last_rows(E, tau, h):
                expert_acts(E, tau)
                for s in range(TURN):
                    add_row(E, tau, s, h)

            front(S, lambda *_: None)
            dve.wait_ge(S.key_read, NCH)
            dve.wait_ge(made, CONSTS)
            for stage_ in pick(S, 0, xTs_flat, rows[:, 0, :]):
                stage_()
            dve.sem_inc(ES.u_free, len(ES.urow))
            dve.sem_inc(ES.v_free, len(ES.vrow))

            turns_done, in_loop = [0], [0]

            def s_turns(where, i=None):
                if where in NO_TURN:
                    return
                if i is None:
                    expert_turn(ES, turns_done[0], S.xn2[:, 0, :], S.h[:, 0, :], first=turns_done[0] == 0)
                    turns_done[0] += 1
                else:
                    expert_turn(ES, i * 3 + (turns_done[0] + in_loop[0]), S.xn2[:, 0, :], S.h[:, 0, :])
                    in_loop[0] += 1
                    if in_loop[0] == 3:
                        in_loop[0] = 0
                        turns_done[0] += 3 * NCH

            front(R, s_turns)
            dve.wait_ge(R.key_read, 2 * NCH)
            first, second = xTr_flat[:, 0:D], xTr_flat[:, D:2 * D]
            stages = pick(R, 1, first, second)
            assert TURNS - turns_done[0] == 4
            for k, stage_ in enumerate(stages):
                stage_()
                if k in (2, 4, 6, 8):
                    s_turns(10)
            dve.sem_inc(ER.u_free, len(ER.urow))
            last_rows(ES, TURNS, S.h[:, 0, :])
            dve.sem_inc(ER.v_free, len(ER.vrow))
            stages = pick(R, 2, first, second)
            assert len(stages) == PEELED - 1
            expert_turn(ER, 0, R.xn2[:, 0, :], R.h[:, 0, :], first=True)
            for tau in range(1, PEELED):
                stages[tau - 1]()
                expert_turn(ER, tau, R.xn2[:, 0, :], R.h[:, 0, :])
            with dve.Fori(PEELED, TURNS) as tau:
                expert_turn(ER, tau, R.xn2[:, 0, :], R.h[:, 0, :])
            expert_acts(ER, TURNS)
            for s in range(TURN):
                dve.wait_ge(ER.u_loaded[s], 16 * (TURNS + 1))
                dve.scalar_tensor_tensor(ER.urow[s], ER.urow[s], 1.0, R.xn2[:, 1, :], ALU.mult, ALU.mult,
                                         accum_out=dots[:, s:s + 1]).then_inc(ER.u_free, 1)
                add_row(ER, TURNS, s, R.h[:, 0, :])
            with dve.Fori(TURNS + 1, 2 * TURNS) as tau:
                expert_turn(ER, tau, R.xn2[:, 1, :], R.h[:, 1, :])
            last_rows(ER, 2 * TURNS, R.h[:, 1, :])


def kernel(x_prompt, x_sample, cache_a_k, cache_a_v, cache_b_k, cache_b_v, cache_b_lf, ln1, w_in, b_f,
           qn_a, kn_a, qn_b, kn_b, rel_bias, w_br_a, w_br_b, w_out, ln2, w_pq, sub_keys, peer_u, peer_v):
    import numpy as np
    import concourse.bacc as bacc
    from concourse.bass_utils import run_bass_kernel_spmd

    def tidy(z):
        return np.ascontiguousarray(z)

    x = np.concatenate([np.asarray(x_prompt)[0], np.asarray(x_sample).reshape(P, D)], axis=0)
    w_in0 = np.asarray(w_in)[0]
    table = np.asarray(rel_bias)[0]
    q, k = np.arange(P)[:, None], np.arange(P)[None, :]

    def spread(distance):
        return tidy(table[:, np.clip(distance, -P, P) + P].transpose(1, 0, 2).reshape(P, HEADS * P))

    def turned(z):
        return tidy(z.T.reshape(KT, P, -1).transpose(1, 0, 2).reshape(P, -1))

    def keys(c):
        return tidy(np.asarray(c)[0].transpose(3, 2, 0, 1).reshape(P, HEADS * STREAMS * P))

    def values(c):
        return tidy(np.asarray(c)[0].transpose(1, 2, 0, 3).reshape(P, HEADS * STREAMS * P))

    ins = {
        "x": x,
        "xTr": turned(x[:2 * P]), "xTs": turned(x[2 * P:]),
        "ln1": tidy(np.asarray(ln1)[0].reshape(KT, P).T),
        "ln2": tidy(np.asarray(ln2)[0]),
        "b_f": tidy(np.asarray(b_f)[0]),
        "w_f": tidy(w_in0[:, FCOL:GCOL].reshape(KT, P, HEADS).transpose(1, 0, 2).reshape(P, KT * HEADS)),
        "w_in": w_in0,
        "clf": tidy(np.asarray(cache_b_lf)[0].transpose(1, 2, 0).reshape(P, HEADS * STREAMS)),
        "subT": tidy(np.asarray(sub_keys)[0].transpose(2, 0, 1).reshape(P, 2 * P)),
        "qn_a": np.asarray(qn_a)[0], "kn_a": np.asarray(kn_a)[0],
        "qn_b": np.asarray(qn_b)[0], "kn_b": np.asarray(kn_b)[0],
        "relD": spread(q - k), "relL": spread(P + q - k), "relC": spread(P + q % SQ - k),
        "ckT_a": keys(cache_a_k), "ckT_b": keys(cache_b_k),
        "cv_a": values(cache_a_v), "cv_b": values(cache_b_v),
        "w_br_a": np.asarray(w_br_a)[0], "w_br_b": np.asarray(w_br_b)[0],
        "w_out": np.asarray(w_out)[0], "w_pq": np.asarray(w_pq)[0],
        "peer_u": np.asarray(peer_u)[0], "peer_v": np.asarray(peer_v)[0],
    }
    outs = {"y": (T, D), "k_a": (T, WIDTH), "v_a": (T, WIDTH), "k_b": (T, WIDTH), "v_b": (T, WIDTH), "lf": (T, HEADS)}
    nc = bacc.Bacc("TRN2", target_bir_lowering=False, num_devices=1)
    arrays, aps = {}, {}
    for name, z in ins.items():
        arrays[f"in_{name}"] = np.ascontiguousarray(z)
        aps[name] = nc.dram_tensor(f"in_{name}", z.shape, F32, kind="ExternalInput").ap()
    for name, shape in outs.items():
        aps[name] = nc.dram_tensor(f"out_{name}", shape, F32, kind="ExternalOutput").ap()
    build(nc, aps)
    r = run_bass_kernel_spmd(nc, [arrays], core_ids=[0]).results[0]
    got = {name: np.asarray(r[f"out_{name}"]) for name in outs}
    S = TT * P - P

    def prompt(z, *rest):
        return z[:S].reshape(1, 1, S, *rest)

    def sample(z, *rest):
        return z[S:].reshape(1, STREAMS, SQ, *rest)

    hd = (HEADS, P)
    return (got["y"][:S].reshape(1, S, D), got["y"][S:].reshape(STREAMS, SQ, D),
            prompt(got["k_a"], *hd), prompt(got["v_a"], *hd), sample(got["k_a"], *hd), sample(got["v_a"], *hd),
            prompt(got["k_b"], *hd), prompt(got["v_b"], *hd), prompt(got["lf"], HEADS),
            sample(got["k_b"], *hd), sample(got["v_b"], *hd), sample(got["lf"], HEADS))
```

```python
from contextlib import ExitStack

import concourse.bass as bass
from concourse import mybir

F32 = mybir.dt.float32
U32 = mybir.dt.uint32
ALU = mybir.AluOpType
ACT = mybir.ActivationFunctionType
AX = mybir.AxisListType.X

P = 128
D = 2048
KT = D // P
TT = 3
T = TT * P
CW = 512
HC = CW // P
NCH = D // CW
KP = 4
NP = KT // KP
HEADS = 8
GROUPS = HEADS // HC
WIDTH = HEADS * P
STREAMS = 8
SQ = P // STREAMS
CHUNK = 64
TOPK = 16
PH = 8
SLOTS = PH * TOPK
TURN = 4
TURNS = SLOTS // TURN
IDX = 4
PEELED = 12
HALVES = ((2, 1, 1, 2, 0), (1, 1, 1, 2, 1), (1, 1, 1, 2, 1), (1, 2, 1, 2, 0))
PASS_TURNS = 2
LATE_TURNS = 5
CONSTS = 15
EPS = 1e-6
ATT_SCALE = float(P) ** -0.5
MASKED = -1e30
FCOL = 6 * WIDTH
GCOL = FCOL + HEADS
CHUNKS = 6 * GROUPS + 5 * NCH
GATES, OUT, PQ = 6 * GROUPS, 6 * GROUPS + 3 * NCH, 6 * GROUPS + 4 * NCH


class Count:

    def __init__(self, sem, by=1):
        self.sem, self.value, self.by = sem, 0, by

    def inc(self, ins):
        ins.then_inc(self.sem, self.by)
        self.value += self.by


class Place:

    def __init__(self):
        self.halves, self.in_pass = 0, 0

    @property
    def turns(self):
        return self.halves // 2

    def first(self, tau):
        return isinstance(tau, int) and tau == 0

    def next(self, halves, i):
        steps = []
        for _ in range(halves):
            tau, half = divmod(self.halves + self.in_pass, 2)
            steps.append((tau if i is None else i * PASS_TURNS + tau, half))
            if i is None:
                self.halves += 1
            else:
                self.in_pass += 1
                if self.in_pass == 2 * PASS_TURNS:
                    self.halves, self.in_pass = self.halves + 2 * PASS_TURNS * NCH, 0
        return steps


class Front:

    def __init__(self, sem, name, tiles, chunk0, streams):
        self.tiles, self.n, self.tokens, self.chunk0, self.streams = tiles, len(tiles), len(tiles) * P, chunk0, streams
        self.v_bank = 1 if streams else 0
        self.blocks = 2 if streams else 3
        self.segments = [(0, 2)] if streams else [(0, 1), (1, 2)]
        self.own = slice(tiles[0], tiles[-1] + 1)
        self.x_loaded = sem(f"x_loaded_{name}")
        self.xT_loaded = sem(f"xT_loaded_{name}")
        self.x_squared = sem(f"x_squared_{name}")
        self.rstd_ready = sem(f"rstd_ready_{name}")
        self.f_done = sem(f"f_done_{name}")
        self.z_each = sem(f"z_each_{name}")
        self.z_ready = sem(f"z_ready_{name}")
        self.z_steps = sem(f"z_steps_{name}")
        self.lf_ready = sem(f"lf_ready_{name}")
        self.xT_scaled = sem(f"xT_scaled_{name}")
        self.proj_read = sem(f"proj_read_{name}")
        self.head_normed = sem(f"head_normed_{name}")
        self.turned = sem(f"turned_{name}")
        self.placed = sem(f"placed_{name}")
        self.lfb_ready = sem(f"lfb_ready_{name}")
        self.st_done = sem(f"st_done_{name}")
        self.st_copied = sem(f"st_copied_{name}")
        self.s_done = sem(f"s_done_{name}")
        self.biased = sem(f"biased_{name}")
        self.max_ready = sem(f"max_ready_{name}")
        self.exp_done = sem(f"exp_done_{name}")
        self.p_ready = sem(f"p_ready_{name}")
        self.pt_done = sem(f"pt_done_{name}")
        self.pt_copied = sem(f"pt_copied_{name}")
        self.y_done = sem(f"y_done_{name}")
        self.y_copied = sem(f"y_copied_{name}")
        self.mix_read = sem(f"mix_read_{name}")
        self.prod_ready = sem(f"prod_ready_{name}")
        self.mixed = sem(f"mixed_{name}")
        self.m_turned = sem(f"m_turned_{name}")
        self.m_placed = sem(f"m_placed_{name}")
        self.x_again = sem(f"x_again_{name}")
        self.h_ready = sem(f"h_ready_{name}")
        self.h_squared = sem(f"h_squared_{name}")
        self.ln2_loaded = sem(f"ln2_loaded_{name}")
        self.xn2_ready = sem(f"xn2_ready_{name}")
        self.n_turned = sem(f"n_turned_{name}")
        self.n_placed = sem(f"n_placed_{name}")
        self.pq_read = sem(f"pq_read_{name}")
        self.pq_turned = sem(f"pq_turned_{name}")
        self.pq_placed = sem(f"pq_placed_{name}")
        self.key_done = sem(f"key_done_{name}")
        self.key_read = sem(f"key_read_{name}")
        self.k_stored = sem(f"k_stored_{name}")
        self.v_stored = sem(f"v_stored_{name}")

    def after(self, c, s=NP - 1):
        return NP * (self.chunk0 + c) + s + 1 + NP


class Experts:

    def __init__(self, sem, name, first, turns, urow, vrow):
        self.name, self.first, self.turns, self.urow, self.vrow = name, first, turns, urow, vrow
        self.u_loaded = [sem(f"u_loaded{n}_{name}") for n in range(len(urow))]
        self.v_loaded = [sem(f"v_loaded{n}_{name}") for n in range(len(vrow))]
        self.u_free = sem(f"u_free_{name}")
        self.v_free = sem(f"v_free_{name}")
        self.gelu_done = sem(f"gelu_done_{name}")
        self.acts_ready = sem(f"acts_ready_{name}")
        self.idx_now = sem(f"idx_now_{name}")


def build(nc, a):
    with ExitStack() as ctx:
        def sb(name, shape, dt=F32):
            return ctx.enter_context(nc.sbuf_tensor(name, shape, dt))

        def sem(name):
            return ctx.enter_context(nc.semaphore(name))

        xTr = sb("xTr", [P, KT, 2 * P])
        xTs = sb("xTs", [P, KT, P])
        wring = sb("wring", [P, NP, KP, CW])
        hr = sb("hr", [P, 2 * D])
        hs = sb("hs", [P, D])
        work = sb("work", [P, 3 * D])
        yTr = sb("yTr", [P, 2 * D])
        yTs = sb("yTs", [P, D])
        xn2s = sb("xn2s", [P, D])
        rows = sb("rows", [P, 4, D])
        stage = sb("stage", [P, 2, CW])
        normed = sb("normed", [P, 2, CW])
        pwork = sb("pwork", [P, 12 * P])
        cst = sb("cst", [P, 2, P])
        clfb = sb("clfb", [P, HC, STREAMS, SQ])
        nmax = sb("nmax", [P, 2, 2])
        rowsum = sb("rowsum", [P, 2, 2])
        rinv = sb("rinv", [P, 2, 2])
        ident = sb("ident", [P, P])
        tri = sb("tri", [P, P])
        ntri = sb("ntri", [P, P])
        stri = sb("stri", [P, P])
        triB = sb("triB", [P, P])
        ntriB = sb("ntriB", [P, P])
        maskC = sb("maskC", [P, P])
        maskO = sb("maskO", [P, P])
        gains = sb("gains", [P, 4, P])
        ln1s = sb("ln1s", [P, KT])
        bfs = sb("bfs", [P, HEADS])
        wf = sb("wf", [P, KT, HEADS])
        lf = sb("lf", [P, TT, HEADS])
        lfw = sb("lfw", [P, 2, TT, HEADS])
        clf = sb("clf", [P, HEADS, STREAMS])
        subT = sb("subT", [P, 2, P])
        ssq = sb("ssq", [P, 2, TT])
        rstd = sb("rstd", [P, 2, TT])
        nwork = sb("nwork", [P, TT])
        hss = sb("hss", [P, 2, HC])
        hrs = sb("hrs", [P, 2, HC])
        hnw = sb("hnw", [P, 2, HC])
        iota16 = sb("iota16", [P, TOPK])
        eidx = sb("eidx", [P, TT, SLOTS], U32)
        gates = sb("gates", [P, TT, SLOTS])
        idxnow = {name: sb(f"idxnow_{name}", [P, IDX, TURN], U32) for name in "sr"}
        dots = sb("dots", [P, TURN])
        gelu = sb("gelu", [P, TURN])
        acts = sb("acts", [P, TURN])
        ps = ctx.enter_context(nc.psum_tensor("ps", [P, 8, CW], F32))

        kval = pwork[:, 0:256].rearrange("p (b k) -> p b k", k=TOPK)
        kidf = pwork[:, 256:512].rearrange("p (b k) -> p b k", k=TOPK)
        kidx = pwork[:, 512:768].bitcast(U32).rearrange("p (b k) -> p b k", k=TOPK)
        cidx = pwork[:, 768:896].bitcast(U32).rearrange("p (h k) -> p h k", k=TOPK)
        cij = pwork[:, 896:1152].bitcast(U32).rearrange("p (s k) -> p s k", s=2)
        cijf = pwork[:, 1152:1408].rearrange("p (s k) -> p s k", s=2)
        bmax = pwork[:, 1408:1416]
        bsum = pwork[:, 1416:1424]

        w_loaded = [sem(f"w_loaded{s}") for s in range(NP)]
        piece_done = sem("piece_done")
        small_loaded = sem("small_loaded")
        ln1_loaded = sem("ln1_loaded")
        made = sem("made")
        biasS_loaded = sem("biasS_loaded")
        biasR_loaded = sem("biasR_loaded")
        masksS_ready = sem("masksS_ready")
        masksR_ready = sem("masksR_ready")
        lf_stored = sem("lf_stored")
        ss_ready = sem("ss_ready")
        root_done = sem("root_done")
        cache_loaded = [sem("ck_loaded"), sem("cv_loaded")]
        best_ready = sem("best_ready")
        gate_exp = sem("gate_exp")
        picked = sem("picked")
        y_stored = sem("y_stored")
        dve_order = sem("dve_order")
        sp_turn = sem("sp_turn")
        pool_turn = sem("pool_turn")

        S = Front(sem, "s", (2,), 0, True)
        R = Front(sem, "r", (0, 1), CHUNKS, False)

        def lay(F, xT, att, y, h, mixed, xn2, prob):
            F.xT, F.h = xT, h
            F.yT = y.rearrange("p (s j n) -> p s j n", s=2, j=HEADS)
            w = HC * F.tokens
            F.qT, F.kT = (att[:, i * w:(i + 1) * w].rearrange("p (j n) -> p j n", j=HC) for i in range(2))
            F.v = att[:, 2 * w:3 * w].rearrange("p (t c) -> p t c", t=F.n)
            F.lfb = att[:, 3 * w:4 * w].rearrange("p (t j n) -> p t j n", t=F.n, j=HC)
            F.mT = mixed[:, 0:KT * F.tokens].rearrange("p (k n) -> p k n", k=KT)
            F.gate = mixed[:, KT * F.tokens:KT * F.tokens + 2 * F.n * CW].rearrange("p (s t c) -> p s t c", s=2, t=F.n)
            F.xn2 = xn2
            F.pkeys = y.rearrange("p (t b n) -> p t b n", t=F.n, b=2 * PH)
            F.pqT = normed[:, 0:F.n, :].rearrange("p t c -> p (t c)").rearrange("p (j n) -> p j n", j=HC)
            F.prob, F.probT = (prob[:, i * 6 * P:i * 6 * P + 2 * F.blocks * P].rearrange("p (w n) -> p w n", w=2)
                               for i in range(2))

        lay(S, xTs, hs[:, :], yTs[:, :], hs[:, :].rearrange("p (t d) -> p t d", t=1), work,
            xn2s[:, :].rearrange("p (t d) -> p t d", t=1), pwork)
        lay(R, xTr, hr[:, :], yTr[:, :], hr[:, :].rearrange("p (t d) -> p t d", t=2), work,
            work[:, 0:2 * D].rearrange("p (t d) -> p t d", t=2), pwork)
        ckT = work[:, 0:2 * D].rearrange("p (j b n) -> p j b n", j=HC, b=STREAMS)
        cv = yTr[:, :].rearrange("p (j b n) -> p j b n", j=HC, b=STREAMS)
        biasS = work[:, 2 * D:3 * D].rearrange("p (w h n) -> p w h n", w=2, h=HEADS)
        biasR = work[:, 0:D].rearrange("p (w h n) -> p w h n", w=2, h=HEADS)
        ln2b = work[:, 2 * D:3 * D]
        S.junk, R.junk = rows[:, 0, :], work[:, 0:D]
        xTs_flat = xTs[:, :, :].rearrange("p k n -> p (k n)")
        xTr_flat = xTr[:, :, :].rearrange("p k n -> p (k n)")
        wflat = wring[:, :, :, :].rearrange("p a b c -> p a (b c)")
        ES = Experts(sem, "s", 2 * SLOTS, TURNS, [rows[:, n, :] for n in (0, 1)],
                     [rows[:, 2, :], rows[:, 3, :], xTs_flat, yTs[:, :]])
        ER = Experts(sem, "r", 0, 2 * TURNS, [wflat[:, n, :] for n in range(NP)], [rows[:, n, :] for n in range(4)])

        block = ctx.enter_context(nc.Block())

        @block.sync
        def _(sp):
            def chunk(n, pieces):
                for s, (w, k0, col) in enumerate(pieces):
                    sp.wait_ge(piece_done, NP * n + s + 1)
                    if not isinstance(n, int):
                        sp.sem_inc(sp_turn, 1)
                    src = w[k0 * P:(k0 + KP) * P, bass.ds(col, CW)].rearrange("(k p) c -> p k c", p=P)
                    sp.dma_start(wring[:, s, :, :], src).then_inc(w_loaded[s], 16)

            def full(w, col):
                return [(w, KP * s, col) for s in range(NP)]

            sp.dma_start(ln1s[:, :], a["ln1"]).then_inc(ln1_loaded, 16)
            sp.dma_start(xTs[:, :, :], a["xTs"].rearrange("p (k n) -> p k n", k=KT)).then_inc(S.xT_loaded, 16)
            for F in (S, R):
                c0 = F.chunk0
                for G in range(2 * GROUPS):
                    br, g = G // GROUPS, G % GROUPS
                    for c in range(3):
                        chunk(c0 + 3 * G + c, full(a["w_in"], (3 * br + c) * WIDTH + g * CW))
                        if F is S and G == 0 and c == 0:
                            sp.dma_start(S.h, a["x"][2 * P:T, :].rearrange("(t p) d -> p t d", p=P)
                                         ).then_inc(S.x_loaded, 16)
                with sp.Fori(0, NCH) as i:
                    n = i * 3 + (c0 + GATES)
                    chunk(n, full(a["w_in"], GCOL + i * CW))
                    chunk(n + 1, full(a["w_in"], GCOL + D + i * CW))
                    chunk(n + 2, [(a["w_br_a"], 0, i * CW), (a["w_br_a"], KP, i * CW),
                                  (a["w_br_b"], 0, i * CW), (a["w_br_b"], KP, i * CW)])
                sp.wait_ge(F.y_copied, 2 * HEADS)
                sp.wait_ge(F.v_stored, 16 * 2 * GROUPS * F.n)
                sp.dma_start(F.h, a["x"][F.tiles[0] * P:(F.tiles[-1] + 1) * P, :].rearrange("(t p) d -> p t d", p=P)
                             ).then_inc(F.x_again, 16)
                with sp.Fori(0, NCH) as i:
                    chunk(i + (c0 + OUT), full(a["w_out"], i * CW))
                sp.wait_ge(F.mixed, F.n * NCH)
                sp.dma_start(ln2b, a["ln2"].partition_broadcast(P)).then_inc(F.ln2_loaded, 16)
                with sp.Fori(0, NCH) as i:
                    chunk(i + (c0 + PQ), full(a["w_pq"], i * CW))
            sp.wait_ge(ES.v_free, len(ES.vrow) + SLOTS)
            sp.dma_start(a["y"][2 * P:T, :], hs[:, :]).then_inc(y_stored, 16)
            for t in range(2):
                sp.wait_ge(ER.v_free, len(ER.vrow) + SLOTS * (t + 1))
                sp.dma_start(a["y"][t * P:(t + 1) * P, :], R.h[:, t, :]).then_inc(y_stored, 16)
            sp.wait_ge(y_stored, 16 * TT)

        @block.gpsimd
        def _(pool):
            order = Count(made)

            def link(ins):
                order.inc(ins)
                pool.wait_ge(made, order.value)

            def select(m, keep, base, pattern, rows_by, fill):
                return pool.affine_select(out=m, in_=m, compare_op=keep, fill=fill, base=base, pattern=pattern,
                                          channel_multiplier=rows_by)

            for dst, src in ((bfs[:, :], a["b_f"].partition_broadcast(P)),
                             (wf[:, :, :], a["w_f"].rearrange("p (k h) -> p k h", k=KT)),
                             (clf[:, :, :], a["clf"].rearrange("p (h b) -> p h b", h=HEADS)),
                             (subT[:, :, :], a["subT"].rearrange("p (s n) -> p s n", s=2)),
                             (gains[:, 0, :], a["qn_a"].partition_broadcast(P)),
                             (gains[:, 1, :], a["kn_a"].partition_broadcast(P)),
                             (gains[:, 2, :], a["qn_b"].partition_broadcast(P)),
                             (gains[:, 3, :], a["kn_b"].partition_broadcast(P))):
                pool.dma_start(dst, src).then_inc(small_loaded, 16)

            link(pool.memset(ident[:, :], 0.0))
            link(select(ident[:, :], ALU.not_equal, 0, [[-1, P]], 1, 1.0))
            link(pool.memset(tri[:, :], 1.0))
            link(select(tri[:, :], ALU.is_ge, 0, [[1, P]], -1, 0.0))
            link(pool.memset(stri[:, :], 1.0))
            link(select(stri[:, :], ALU.is_gt, 0, [[-1, P]], 1, 0.0))
            starts, ends = [[-SQ, STREAMS], [0, SQ]], [[SQ, STREAMS], [0, SQ]]
            link(pool.tensor_copy(triB[:, :], tri[:, :]))
            link(select(triB[:, :].rearrange("p (b n) -> p b n", b=STREAMS), ALU.is_ge, 0, starts, 1, 0.0))
            link(pool.tensor_scalar_mul(ntri[:, :], tri[:, :], -1.0))
            link(pool.tensor_scalar_mul(ntriB[:, :], triB[:, :], -1.0))
            link(pool.iota(iota16[:, :], pattern=[[1, TOPK]], base=0, channel_multiplier=0,
                           allow_small_or_imprecise_dtypes=True))
            link(pool.memset(maskC[:, :], 0.0))
            link(select(maskC[:, :], ALU.is_ge, 0, [[-1, P]], 1, MASKED))
            link(pool.tensor_copy(maskO[:, :], maskC[:, :]))
            link(select(maskO[:, :].rearrange("p (b n) -> p b n", b=STREAMS), ALU.is_gt, SQ, ends, -1, MASKED))
            assert order.value == CONSTS

            for w, rel in enumerate(("relC", "relD")):
                pool.dma_start(biasS[:, w, :, :], a[rel].rearrange("p (h n) -> p h n", h=HEADS)
                               ).then_inc(biasS_loaded, 16)

            def load_caches(G):
                half = HC * STREAMS * P
                lo = (G % GROUPS) * half
                k, w = (("ckT_a", "cv_a"), ("ckT_b", "cv_b"))[G // GROUPS]
                for sm, dst, src, used in ((cache_loaded[0], ckT, a[k], S.st_done), (cache_loaded[1], cv, a[w], S.y_done)):
                    if G:
                        pool.wait_ge(used, HC * G)
                    pool.dma_start(dst, src[:, lo:lo + half].rearrange("p (j b n) -> p j b n", j=HC, b=STREAMS)
                                   ).then_inc(sm, 16)

            load_caches(0)
            pool.wait_ge(biasS_loaded, 32)
            own = biasS[:, 1, :, :].rearrange("p h (b n) -> p h b n", b=STREAMS)
            link(select(own, ALU.is_ge, 0, [[0, HEADS]] + starts, 1, MASKED))
            select(own, ALU.is_gt, SQ, [[0, HEADS]] + ends, -1, MASKED).then_inc(masksS_ready, 1)

            for G in range(2 * GROUPS):
                if G:
                    load_caches(G)
                if G == 1:
                    pool.dma_start(R.h, a["x"][0:2 * P, :].rearrange("(t p) d -> p t d", p=P)).then_inc(R.x_loaded, 16)
                if G == 2:
                    pool.dma_start(xTr[:, :, :], a["xTr"].rearrange("p (k n) -> p k n", k=KT)).then_inc(R.xT_loaded, 16)
                br, cols = "ab"[G // GROUPS], slice((G % GROUPS) * CW, (G % GROUPS + 1) * CW)
                pool.wait_ge(S.head_normed, 2 * G + 2)
                pool.dma_start(a[f"k_{br}"][2 * P:T, cols], normed[:, 0, :]).then_inc(S.k_stored, 16)
                pool.wait_ge(S.proj_read, 3 * G + 3)
                pool.dma_start(a[f"v_{br}"][2 * P:T, cols], S.v[:, 0, :]).then_inc(S.v_stored, 16)

            pool.wait_ge(S.h_ready, NCH)
            for w, rel in enumerate(("relL", "relD")):
                pool.dma_start(biasR[:, w, :, :], a[rel].rearrange("p (h n) -> p h n", h=HEADS)
                               ).then_inc(biasR_loaded, 16)
            pool.wait_ge(biasR_loaded, 32)
            select(biasR[:, 1, :, CHUNK:P], ALU.is_ge, -CHUNK, [[0, HEADS], [0, P - CHUNK]], 1,
                   MASKED).then_inc(masksR_ready, 1)

            eflat = eidx[:, :, :].rearrange("p t s -> p (t s)")

            def gather(E, table, row, loaded, free, count, col):
                pool.wait_ge(free, count)
                pool.sem_inc(pool_turn, 1)
                pool.indirect_dma_start(row, None, table[:, :], bass.IndirectOffsetOnAxis(ap=col, axis=0)
                                        ).then_inc(loaded, 16)

            def turn(E, tau, at, first=False):
                if not first:
                    pool.wait_ge(E.u_free, tau * TURN)
                    pool.sem_inc(pool_turn, 1)
                pool.tensor_copy(idxnow[E.name][:, at, :], eflat[:, bass.ds(tau * TURN + E.first, TURN)]).then_inc(E.idx_now, 1)
                pool.wait_ge(E.idx_now, tau + 1)
                NU, NV = len(E.urow), len(E.vrow)
                for s in range(TURN):
                    gather(E, a["peer_u"], E.urow[s % NU], E.u_loaded[s % NU], E.u_free, tau * TURN + s + 1,
                           idxnow[E.name][:, at, s:s + 1])
                    if not first:
                        gather_v(E, tau - 1, (at - 1) % IDX, s)

            def gather_v(E, tau, at, s):
                NV = len(E.vrow)
                gather(E, a["peer_v"], E.vrow[s % NV], E.v_loaded[s % NV], E.v_free, tau * TURN + s + 1,
                       idxnow[E.name][:, at, s:s + 1])

            for E, ready in ((ES, 1), (ER, 2)):
                pool.wait_ge(picked, ready)
                turn(E, 0, 0, first=True)
                for tau in range(1, IDX):
                    turn(E, tau, tau)

                def body(m):
                    for q in range(IDX):
                        turn(E, m * IDX + q, q)

                if E is ES:
                    with pool.Fori(1, E.turns // IDX) as m:
                        body(m)
                else:
                    with pool.Fori(1, TURNS // IDX) as m:
                        body(m)
                    pool.wait_ge(picked, 3)
                    with pool.Fori(TURNS // IDX, E.turns // IDX) as m:
                        body(m)
                for s in range(TURN):
                    gather_v(E, E.turns - 1, IDX - 1, s)
            pool.wait_ge(S.k_stored, 16 * 2 * GROUPS)
            pool.wait_ge(R.k_stored, 16 * 2 * GROUPS * 2)
            pool.wait_ge(lf_stored, 16)

        @block.tensor
        def _(pe):
            mm = pe.matmul
            sk = dict(skip_group_check=True)
            pe.sem_inc(piece_done, NP)

            def part(F, n, s, src, k0, bank, kt=KT):
                pe.wait_ge(w_loaded[s], (n + 1) * 16)
                for k in range(KP):
                    for t in range(F.n):
                        last = mm(ps[:, bank + t, :], src[:, k0 + k, t * P:(t + 1) * P], wring[:, s, k, :],
                                  start=(k0 + k == 0), stop=(k0 + k == kt - 1))
                last.then_inc(piece_done, 1)

            def chunk(F, n, src, bank):
                for s in range(NP):
                    part(F, n, s, src, KP * s, bank)

            def turn_tiles(F, u0, ready, done, read, src):
                for t in range(F.n):
                    u = u0 + t
                    pe.wait_ge(ready, u + 1)
                    if u >= 2:
                        pe.wait_ge(read, u - 1)
                    for j in range(HC):
                        last = pe.transpose(ps[:, 6 + u % 2, j * P:(j + 1) * P], src(t)[:, j * P:(j + 1) * P],
                                            ident[:, :])
                    last.then_inc(done, 1)

            def group(F, G, fill):
                br, H0, n, c0 = G // GROUPS, HC * G, F.n, F.chunk0
                if G == 0:
                    chunk(F, c0 + 3 * G, F.xT, 0)
                    chunk(F, c0 + 3 * G + 1, F.xT, 2)
                if not F.streams:
                    pe.wait_ge(F.proj_read, 3 * n * G + n)
                part(F, c0 + 3 * G + 2, 0, F.xT, 0, F.v_bank)
                part(F, c0 + 3 * G + 2, 1, F.xT, KP, F.v_bank)
                if G == 1:
                    forget_gate(F)
                if G:
                    pe.wait_ge(F.pt_copied, H0)
                    pe.wait_ge(F.y_copied, H0)
                else:
                    pe.wait_ge(made, CONSTS)
                turn_tiles(F, 2 * n * G, F.head_normed, F.turned, F.placed, lambda t: normed[:, t, :])
                part(F, c0 + 3 * G + 2, 2, F.xT, 2 * KP, F.v_bank)
                part(F, c0 + 3 * G + 2, 3, F.xT, 3 * KP, F.v_bank)
                turn_tiles(F, 2 * n * G + n, F.head_normed, F.turned, F.placed, lambda t: normed[:, t, :])
                pe.wait_ge(F.proj_read, 3 * n * (G + 1))
                fill()
                pe.wait_ge(F.placed, 2 * n * (G + 1))
                if br:
                    pe.wait_ge(F.lfb_ready, G - GROUPS + 1)
                if F.streams:
                    pe.wait_ge(cache_loaded[0], 16 * (G + 1))

                def q_of(j, t):
                    return F.qT[:, j, t * P:(t + 1) * P]

                def cached_scores(j):
                    if H0 + j:
                        pe.wait_ge(F.st_copied, H0 + j)
                    out = ps[:, 3, 0:P]
                    if br:
                        mm(out, stri[:, :], clfb[:, j, :, :].rearrange("p b n -> p (b n)"), start=True, stop=True)
                    for b in range(STREAMS):
                        last = mm(out[:, b * SQ:(b + 1) * SQ], ckT[:, j, b, :], q_of(j, 0)[:, b * SQ:(b + 1) * SQ],
                                  start=(not br and b == 0), stop=True, **sk)
                    last.then_inc(F.st_done, 1)

                def scores(j):
                    H = H0 + j
                    if H >= 2:
                        pe.wait_ge(F.biased, H - 1)
                    A = ps[:, 4 + j % 2, :]
                    if F.streams:
                        mm(A[:, P:2 * P], q_of(j, 0), F.kT[:, j, :], start=True, stop=True, **sk)
                        f = F.lfb[:, 0, j, :] if br else None
                        extra = ((1, f, ntriB), (1, triB, f), (0, triB, f)) if br else ()
                    else:
                        mm(A[:, 0:P], q_of(j, 0), F.kT[:, j, 0:P], start=True, stop=True, **sk)
                        mm(A[:, P:3 * P], q_of(j, 1), F.kT[:, j, :], start=False, stop=True, **sk)
                        f0, f1 = (F.lfb[:, t, j, :] for t in range(2)) if br else (None, None)
                        extra = ((0, f0, ntri), (0, tri, f0), (1, f0, stri), (1, tri, f1), (2, f1, ntri),
                                 (2, tri, f1)) if br else ()
                    last = None
                    for m, left, right in extra:
                        last = mm(A[:, m * P:(m + 1) * P], left[:, :], right[:, :], start=False, stop=True, **sk)
                    if F.streams:
                        pe.wait_ge(F.st_copied, H + 1)
                        last = mm(A[:, 0:P], cst[:, j % 2, :], ident[:, :], start=False, stop=True, **sk)
                    elif last is None:
                        last = mm(A[:, 3 * P:3 * P + 1], ident[:, :], ident[:, 0:1], start=False, stop=True, **sk)
                    last.then_inc(F.s_done, 1)

                def turn_probs(j):
                    H = H0 + j
                    pe.wait_ge(F.p_ready, H + 1)
                    if H:
                        pe.wait_ge(F.pt_copied, H)
                    for m in range(F.blocks):
                        last = pe.transpose(ps[:, 6, m * P:(m + 1) * P], F.prob[:, j % 2, m * P:(m + 1) * P],
                                            ident[:, :])
                    last.then_inc(F.pt_done, 1)

                def values(j):
                    H = H0 + j
                    pe.wait_ge(F.pt_copied, H + 1)
                    if H:
                        pe.wait_ge(F.y_copied, H)
                    Y = ps[:, 7, :]

                    def pt(m):
                        return F.probT[:, j % 2, m * P:(m + 1) * P]

                    def vh(t):
                        return F.v[:, t, j * P:(j + 1) * P]
                    if F.streams:
                        pe.wait_ge(cache_loaded[1], 16 * (G + 1))
                        mm(Y[:, 0:P], vh(0), pt(1), start=True, stop=True, **sk)
                        for b in range(STREAMS):
                            last = mm(Y[:, b * SQ:(b + 1) * SQ], cv[:, j, b, :], pt(0)[:, b * SQ:(b + 1) * SQ],
                                      start=False, stop=True, **sk)
                    else:
                        mm(Y[:, 0:P], vh(0), pt(0), start=True, stop=True, **sk)
                        mm(Y[:, P:2 * P], vh(0), pt(1), start=False, stop=True, **sk)
                        last = mm(Y[:, P:2 * P], vh(1), pt(2), start=False, stop=True, **sk)
                    last.then_inc(F.y_done, 1)

                def score(j):
                    if F.streams:
                        cached_scores(j)
                    scores(j)

                score(0)
                if G == 1:
                    pe.wait_ge(F.z_ready, 1)
                score(1)
                fill()
                for j in range(HC):
                    turn_probs(j)
                    if j + 2 < HC:
                        if F.streams:
                            cached_scores(j + 2)
                    fill()
                    values(j)
                    if j + 2 < HC:
                        scores(j + 2)
                        fill()

            def forget_gate(F):
                pe.wait_ge(small_loaded, 16 * 8)
                pe.wait_ge(F.biased, HC)
                for t in range(F.n):
                    col = (F.tiles[0] + t) * HEADS
                    for k in range(KT):
                        last = mm(ps[:, 5, col:col + HEADS], F.xT[:, k, t * P:(t + 1) * P], wf[:, k, :],
                                  start=(k == 0), stop=(k == KT - 1))
                last.then_inc(F.f_done, 1)

            def front(F):
                n, c0 = F.n, F.chunk0
                pe.wait_ge(F.xT_scaled, 1)
                for G in range(2 * GROUPS):
                    pieces = iter([(c, s) for c in range(2) for s in range(NP)])

                    def fill():
                        c, s = next(pieces)
                        part(F, c0 + 3 * (G + 1) + c, s, F.xT, KP * s, 2 * c)

                    group(F, G, fill)
                    assert next(pieces, None) is None

                pe.wait_ge(F.y_copied, 2 * HEADS)
                pe.wait_ge(F.pt_copied, 2 * HEADS)

                def gates_and_branches(i, filled=False):
                    g0 = c0 + GATES
                    read = 3 * n * 2 * GROUPS
                    if not filled:
                        pe.wait_ge(F.mix_read, i * (2 * n) + n)
                        chunk(F, i * 3 + g0, F.xT, 0)
                        pe.wait_ge(F.mix_read, i * (2 * n) + 2 * n)
                        chunk(F, i * 3 + (g0 + 1), F.xT, 2)
                    pe.wait_ge(F.proj_read, i * (2 * n) + (read + n))
                    part(F, i * 3 + (g0 + 2), 0, F.yT[:, 0, :, :], 0, 0, HEADS)
                    part(F, i * 3 + (g0 + 2), 1, F.yT[:, 0, :, :], KP, 0, HEADS)
                    pe.wait_ge(F.proj_read, i * (2 * n) + (read + 2 * n))
                    part(F, i * 3 + (g0 + 2), 2, F.yT[:, 1, :, :], 0, 2, HEADS)
                    part(F, i * 3 + (g0 + 2), 3, F.yT[:, 1, :, :], KP, 2, HEADS)
                    for t in range(n):
                        pe.wait_ge(F.mixed, i * n + t + 1)
                        pe.wait_ge(F.m_placed, i * n + t + 1)
                        for j in range(HC):
                            last = pe.transpose(ps[:, 6 + t % 2, j * P:(j + 1) * P], stage[:, t, j * P:(j + 1) * P],
                                                ident[:, :])
                        last.then_inc(F.m_turned, 1)

                gates_and_branches(0, True)
                with pe.Fori(1, NCH) as i:
                    gates_and_branches(i)
                pe.wait_ge(F.m_placed, n * NCH + n)
                for i in range(NCH):
                    if i >= 2:
                        pe.wait_ge(F.h_ready, n * (i - 1))
                    chunk(F, c0 + OUT + i, F.mT, 2 * (i % 2))
                for t in range(n):
                    pe.wait_ge(F.xn2_ready, t + 1)
                    for q in range(KT // HC):
                        c = t * (KT // HC) + q
                        if c >= 2:
                            pe.wait_ge(F.n_placed, c - 1)
                        for j in range(HC):
                            last = pe.transpose(ps[:, 6 + c % 2, j * P:(j + 1) * P],
                                                F.xn2[:, t, (q * HC + j) * P:(q * HC + j + 1) * P], ident[:, :])
                        last.then_inc(F.n_turned, 1)
                pe.wait_ge(F.n_placed, n * KT // HC)
                pe.wait_ge(F.h_ready, n * NCH)

                def keys(i):
                    turn_tiles(F, n * i, F.pq_read, F.pq_turned, F.pq_placed, lambda t: stage[:, t, :])
                    for t in range(n):
                        u = n * i + t
                        pe.wait_ge(F.pq_placed, u + 1)
                        if u >= 2:
                            pe.wait_ge(F.key_read, u - 1)
                        for j in range(HC):
                            last = mm(ps[:, 4 + u % 2, j * P:(j + 1) * P], F.pqT[:, j, t * P:(t + 1) * P],
                                      subT[:, j % 2, :], start=(j == 0), stop=True, **sk)
                        last.then_inc(F.key_done, 1)

                for i in range(NCH):
                    if i >= 2:
                        pe.wait_ge(F.pq_read, n * (i - 1))
                    chunk(F, c0 + PQ + i, F.xT, 2 * (i % 2))
                    if i:
                        keys(i - 1)
                keys(NCH - 1)

            front(S)
            front(R)

        @block.scalar
        def _(act):
            roots = [0]

            def root(v):
                roots[0] += 1
                act.wait_ge(ss_ready, roots[0])
                act.activation(v, v, ACT.Sqrt).then_inc(root_done, 1)

            def expert_gelu(E, tau):
                act.wait_ge(E.u_free, tau * TURN + (TURN + len(E.urow)))
                if not (isinstance(tau, int) and tau == 0):
                    act.wait_ge(E.acts_ready, tau)
                act.activation(gelu[:, :], dots[:, :], ACT.Gelu).then_inc(E.gelu_done, 1)

            act.sem_inc(S.m_placed, S.n)
            act.sem_inc(R.m_placed, R.n)
            def prepare(F):
                act.wait_ge(F.x_loaded, 16)
                for t in range(F.n):
                    act.activation(S.junk, F.h[:, t, :], ACT.Square,
                                   accum_out=ssq[:, 0, F.tiles[t]:F.tiles[t] + 1]).then_inc(F.x_squared, 1)
                    act.wait_ge(F.x_squared, t + 1)
                root(rstd[:, 0, F.own])
                act.wait_ge(F.rstd_ready, 1)

            def log_sigmoid(F):
                z, w = lfw[:, 0, F.own, :], lfw[:, 1, F.own, :]
                act.wait_ge(F.z_ready, 1)
                act.activation(w, z, ACT.Abs).then_inc(F.z_steps, 1)
                act.wait_ge(F.z_steps, 1)
                act.activation(w, w, ACT.Exp, scale=-1.0).then_inc(F.z_steps, 1)
                act.wait_ge(F.z_steps, 2)
                act.activation(w, w, ACT.Ln, bias=1.0).then_inc(F.z_steps, 1)

            def front(F, experts):
                n, t0 = F.n, F.tiles[0]

                def blocks(bank):
                    return ps[:, bank, :].rearrange("p (j n) -> p j n", j=HC)

                def place(u0, dst, turned, placed):
                    for t in range(n):
                        act.wait_ge(turned, u0 + t + 1)
                        act.activation(dst[:, :, t * P:(t + 1) * P], blocks(6 + (u0 + t) % 2), ACT.Copy
                                       ).then_inc(placed, 1)

                def scale(t):
                    return rstd[:, 0, t0 + t:t0 + t + 1]

                for G in range(2 * GROUPS):
                    H0, br, cols = HC * G, "ab"[G // GROUPS], slice((G % GROUPS) * CW, (G % GROUPS + 1) * CW)
                    for c in range(2):
                        act.wait_ge(piece_done, F.after(3 * G + c))
                        for t in range(n):
                            u = 2 * n * G + n * c + t
                            if u >= n:
                                act.wait_ge(F.head_normed, u - n + 1)
                            act.activation(stage[:, t, :], ps[:, 2 * c + t, :], ACT.Copy, scale=scale(t)
                                           ).then_inc(F.proj_read, 1)
                        if c:
                            place(2 * n * G, F.qT, F.turned, F.placed)
                        if G and c == 0:
                            experts(HALVES[G - 1][4])
                        root(hrs[:, 0:n, :])
                        experts(HALVES[G][c])
                    act.wait_ge(piece_done, F.after(3 * G + 2))
                    if G:
                        act.wait_ge(F.v_stored, 16 * n * G)
                    for t in range(n):
                        act.activation(F.v[:, t, :], ps[:, F.v_bank + t, :], ACT.Copy, scale=scale(t)).then_inc(F.proj_read, 1)
                    place(2 * n * G + n, F.kT, F.turned, F.placed)
                    if not F.streams:
                        act.wait_ge(F.head_normed, 2 * n * (G + 1))
                        act.wait_ge(F.proj_read, 3 * n * (G + 1))
                        for t in range(n):
                            rows_ = slice((t0 + t) * P, (t0 + t + 1) * P)
                            if G == 2 and t == 0:
                                act.wait_ge(S.lf_ready, 1)
                                act.wait_ge(R.lf_ready, 1)
                                act.dma_start(a["lf"].rearrange("(t p) h -> p t h", p=P), lf[:, :, :]
                                              ).then_inc(lf_stored, 16)
                            act.dma_start(a[f"k_{br}"][rows_, cols], normed[:, t, :]).then_inc(F.k_stored, 16)
                            act.dma_start(a[f"v_{br}"][rows_, cols], F.v[:, t, :]).then_inc(F.v_stored, 16)

                    def copy_cached(j):
                        if F.streams:
                            act.wait_ge(F.st_done, H0 + j + 1)
                            act.activation(cst[:, j % 2, :], ps[:, 3, 0:P], ACT.Copy).then_inc(F.st_copied, 1)

                    def exps(j):
                        act.wait_ge(F.max_ready, H0 + j + 1)
                        for w, (m, k) in enumerate(F.segments):
                            x = F.prob[:, j % 2, m * P:(m + k) * P]
                            last = act.activation(x, x, ACT.Exp, bias=nmax[:, j % 2, w:w + 1],
                                                  accum_out=rowsum[:, j % 2, w:w + 1])
                        last.then_inc(F.exp_done, 1)

                    def copy_probs(j):
                        act.wait_ge(F.pt_done, H0 + j + 1)
                        act.activation(F.probT[:, j % 2, :], ps[:, 6, 0:F.blocks * P], ACT.Copy
                                       ).then_inc(F.pt_copied, 1)

                    def copy_y(j):
                        H = H0 + j
                        act.wait_ge(F.y_done, H + 1)
                        act.activation(F.yT[:, H // HEADS, H % HEADS, :], ps[:, 7, 0:F.tokens], ACT.Copy
                                       ).then_inc(F.y_copied, 1)

                    if G == 1:
                        log_sigmoid(F)
                    copy_cached(0)
                    copy_cached(1)
                    exps(0)
                    exps(1)
                    for j in range(HC):
                        copy_probs(j)
                        if j + 2 < HC:
                            copy_cached(j + 2)
                        copy_y(j)
                        if j + 2 < HC:
                            experts(HALVES[G][2 + j])
                            exps(j + 2)
                    if F is S and G == 2:
                        prepare(R)

                with act.Fori(0, NCH) as i:
                    for s in range(2):
                        act.wait_ge(piece_done, i * (3 * NP) + F.after(GATES + s))
                        act.wait_ge(F.mix_read, i * (2 * n) + n * (s + 1))
                        for t in range(n):
                            act.activation(F.gate[:, s, t, :], ps[:, 2 * s + t, :], ACT.Sigmoid, scale=scale(t)
                                           ).then_inc(F.proj_read, 1)
                        if s == 0:
                            experts(2, i)
                    for t in range(n):
                        act.wait_ge(F.m_turned, i * n + t + 1)
                        act.activation(F.mT[:, bass.ds(i * HC, HC), t * P:(t + 1) * P], blocks(6 + t % 2), ACT.Copy
                                       ).then_inc(F.m_placed, 1)
                    experts(2, i)
                for i in range(NCH):
                    experts(1)
                act.wait_ge(F.h_ready, n * NCH)
                for t in range(n):
                    act.activation(F.junk, F.h[:, t, :], ACT.Square, accum_out=ssq[:, 1, t0 + t:t0 + t + 1]
                                   ).then_inc(F.h_squared, 1)
                    act.wait_ge(F.h_squared, t + 1)
                root(rstd[:, 1, t0:t0 + n])
                for t in range(n):
                    for q in range(KT // HC):
                        c = t * (KT // HC) + q
                        act.wait_ge(F.n_turned, c + 1)
                        act.activation(F.xT[:, q * HC:(q + 1) * HC, t * P:(t + 1) * P], blocks(6 + c % 2), ACT.Copy
                                       ).then_inc(F.n_placed, 1)
                experts(2)

                def keys(i):
                    for t in range(n):
                        u = n * i + t
                        act.wait_ge(F.pq_turned, u + 1)
                        if i:
                            act.wait_ge(F.key_done, n * i)
                        act.activation(F.pqT[:, :, t * P:(t + 1) * P], blocks(6 + u % 2), ACT.Copy
                                       ).then_inc(F.pq_placed, 1)
                    for t in range(n):
                        u = n * i + t
                        act.wait_ge(F.key_done, u + 1)
                        act.activation(F.pkeys[:, t, i * HC:(i + 1) * HC, :], blocks(4 + u % 2), ACT.Copy
                                       ).then_inc(F.key_read, 1)

                act.wait_ge(F.k_stored, 16 * 2 * GROUPS * n)
                for i in range(NCH):
                    act.wait_ge(piece_done, F.after(PQ + i))
                    for t in range(n):
                        if i:
                            act.wait_ge(F.pq_turned, n * (i - 1) + t + 1)
                        act.activation(stage[:, t, :], ps[:, 2 * (i % 2) + t, :], ACT.Copy).then_inc(F.pq_read, 1)
                    keys(i)
                    experts(2)

            def gate_exps(k):
                t = (2, 0, 1)[k]
                act.wait_ge(best_ready, k + 1)
                act.activation(gates[:, t, :], gates[:, t, :], ACT.Exp).then_inc(gate_exp, 1)

            prepare(S)
            front(S, lambda *_: None)
            gate_exps(0)

            def stream_turns(halves, i=None):
                for tau, half in streams_place.next(halves, i):
                    if half:
                        expert_gelu(ES, tau)

            streams_place = Place()
            front(R, stream_turns)
            for k, tau in enumerate(range(TURNS - LATE_TURNS, TURNS)):
                if k == LATE_TURNS - 1:
                    gate_exps(1)
                expert_gelu(ES, tau)
            for tau in range(PEELED):
                expert_gelu(ER, tau)
                if tau == PEELED - 4:
                    gate_exps(2)
            with act.Fori(PEELED, 2 * TURNS) as tau:
                expert_gelu(ER, tau)

        @block.vector
        def _(dve):
            order, roots = Count(dve_order), Count(root_done)

            def step(ins):
                order.inc(ins)

            def settle():
                dve.wait_ge(dve_order, order.value)

            def link(ins):
                step(ins)
                settle()

            def root(dst, src, work_, width):
                link(dve.tensor_scalar(src, src, 1.0 / width, EPS, ALU.mult, ALU.add))
                dve.reciprocal(dst, src).then_inc(ss_ready, 1)
                roots.value += 1
                dve.wait_ge(root_done, roots.value)
                link(dve.tensor_tensor(work_, dst, dst, ALU.mult))
                link(dve.tensor_tensor(work_, work_, src, ALU.mult))
                link(dve.tensor_scalar(work_, work_, -0.5, 1.5, ALU.mult, ALU.add))
                link(dve.tensor_tensor(dst, dst, work_, ALU.mult))

            dve.sem_inc(S.mix_read, 2 * S.n)
            dve.sem_inc(R.mix_read, 2 * R.n)
            dve.wait_ge(ln1_loaded, 16)

            def prepare(F):
                dve.wait_ge(F.xT_loaded, 16)
                for k in range(KT):
                    last = dve.tensor_scalar(F.xT[:, k, :], F.xT[:, k, :], ln1s[:, k:k + 1], None, ALU.mult)
                last.then_inc(F.xT_scaled, 1)
                if F is S:
                    dve.wait_ge(small_loaded, 16 * 8)
                    for c in (0, 2):
                        link(dve.tensor_scalar(gains[:, c, :], gains[:, c, :], ATT_SCALE, None, ALU.mult))
                dve.wait_ge(F.x_squared, F.n)
                root(rstd[:, 0, F.own], ssq[:, 0, F.own], nwork[:, F.own], D)
                dve.sem_inc(F.rstd_ready, 1)

            def forget_gate(F):
                dve.wait_ge(F.f_done, 1)
                for t in F.tiles:
                    dve.scalar_tensor_tensor(lfw[:, 0, t, :], ps[:, 5, t * HEADS:(t + 1) * HEADS],
                                             rstd[:, 0, t:t + 1], bfs[:, :], ALU.mult, ALU.add).then_inc(F.z_each, 1)
                dve.wait_ge(F.z_each, F.n)
                dve.sem_inc(F.z_ready, 1)
                dve.wait_ge(F.z_steps, 3)
                dve.scalar_tensor_tensor(lf[:, F.own, :], lfw[:, 0, F.own, :], 0.0, lfw[:, 1, F.own, :], ALU.min,
                                         ALU.subtract).then_inc(F.lf_ready, 1)

            def front(F, experts):
                n, t0 = F.n, F.tiles[0]
                for G in range(2 * GROUPS):
                    br, g, H0 = G // GROUPS, G % GROUPS, HC * G
                    for c in range(2):
                        for t in range(n):
                            dve.wait_ge(F.proj_read, 3 * n * G + n * c + t + 1)
                            if c:
                                dve.wait_ge(F.turned, 2 * n * G + t + 1)
                            elif G:
                                dve.wait_ge(F.turned, 2 * n * G - n + t + 1)
                                dve.wait_ge(F.k_stored, 16 * n * G)
                            elif F is R:
                                dve.wait_ge(S.key_done, NCH)
                            link(dve.tensor_tensor(normed[:, t, :], stage[:, t, :], stage[:, t, :], ALU.mult))
                            link(dve.tensor_reduce(hss[:, t, :], normed[:, t, :].rearrange("p (j n) -> p j n", j=HC),
                                                   AX, ALU.add))
                        root(hrs[:, 0:n, :], hss[:, 0:n, :], hnw[:, 0:n, :], P)
                        for t in range(n):
                            for j in range(HC):
                                blk = slice(j * P, (j + 1) * P)
                                last = dve.scalar_tensor_tensor(normed[:, t, blk], stage[:, t, blk],
                                                                hrs[:, t, j:j + 1], gains[:, 2 * br + c, :],
                                                                ALU.mult, ALU.mult)
                            last.then_inc(F.head_normed, 1)
                        experts(HALVES[G][c])
                    if br:
                        dve.wait_ge(F.lf_ready, 1)
                        for j in range(HC):
                            h = HC * g + j
                            for t in range(n):
                                last = dve.tensor_copy(F.lfb[:, t, j, :],
                                                       lf[:, t0 + t, h:h + 1].to_broadcast([P, P]))
                            if F.streams:
                                last = dve.tensor_copy(clfb[:, j, :, :],
                                                       clf[:, h, :].unsqueeze(2).to_broadcast([P, STREAMS, SQ]))
                        last.then_inc(F.lfb_ready, 1)
                    elif G == 0:
                        dve.wait_ge(masksS_ready if F.streams else masksR_ready, 1)

                    def bias(j):
                        H, h = H0 + j, HC * g + j
                        dve.wait_ge(F.s_done, H + 1)
                        if H >= 2:
                            dve.wait_ge(F.pt_done, H - 1)
                        A, X = ps[:, 4 + j % 2, :], F.prob[:, j % 2, :]

                        def two(x):
                            return x.rearrange("p (w n) -> p w n", w=2)
                        if F.streams and not br:
                            dve.tensor_tensor(two(X), two(A[:, 0:2 * P]), biasS[:, :, h, :], ALU.add
                                              ).then_inc(F.biased, 1)
                        elif not br:
                            step(dve.tensor_tensor(X[:, 0:P], A[:, 0:P], biasR[:, 1, h, :], ALU.add))
                            dve.tensor_tensor(two(X[:, P:3 * P]), two(A[:, P:3 * P]), biasR[:, :, h, :], ALU.add
                                              ).then_inc(F.biased, 1)
                        elif F.streams:
                            step(dve.tensor_copy(X[:, 0:P], A[:, 0:P]))
                            dve.tensor_tensor(X[:, P:2 * P], A[:, P:2 * P], maskO[:, :], ALU.add).then_inc(F.biased, 1)
                        else:
                            step(dve.tensor_tensor(X[:, 0:P], A[:, 0:P], maskC[:, :], ALU.add))
                            step(dve.tensor_copy(X[:, P:2 * P], A[:, P:2 * P]))
                            dve.tensor_tensor(X[:, 2 * P:3 * P], A[:, 2 * P:3 * P], maskC[:, :], ALU.add
                                              ).then_inc(F.biased, 1)
                        dve.wait_ge(F.biased, H + 1)
                        for w, (m, k) in enumerate(F.segments):
                            step(dve.tensor_reduce(rinv[:, j % 2, w:w + 1], X[:, m * P:(m + k) * P], AX, ALU.max))
                        settle()
                        dve.tensor_scalar(nmax[:, j % 2, :n], rinv[:, j % 2, :n], -1.0, None, ALU.mult
                                          ).then_inc(F.max_ready, 1)
                        dve.wait_ge(F.max_ready, H + 1)

                    def norm(j):
                        dve.wait_ge(F.exp_done, H0 + j + 1)
                        X = F.prob[:, j % 2, :]
                        link(dve.reciprocal(rinv[:, j % 2, :n], rowsum[:, j % 2, :n]))
                        for w, (m, k) in enumerate(F.segments):
                            x = X[:, m * P:(m + k) * P]
                            last = dve.tensor_scalar(x, x, rinv[:, j % 2, w:w + 1], None, ALU.mult)
                        last.then_inc(F.p_ready, 1)

                    if G == 1:
                        forget_gate(F)
                    bias(0)
                    bias(1)
                    norm(0)
                    norm(1)
                    experts(HALVES[G][2])
                    bias(2)
                    norm(2)
                    experts(HALVES[G][3])
                    bias(3)
                    norm(3)
                    experts(HALVES[G][4])
                    if F is S and G == 2:
                        prepare(R)

                with dve.Fori(0, NCH) as i:
                    experts(2, i)
                    for s in range(2):
                        dve.wait_ge(piece_done, i * (3 * NP) + F.after(GATES + 2, 2 * s + 1))
                        for t in range(n):
                            dve.tensor_tensor(F.gate[:, s, t, :], ps[:, 2 * s + t, :], F.gate[:, s, t, :], ALU.mult
                                              ).then_inc(F.prod_ready, 1)
                    for t in range(n):
                        dve.wait_ge(F.prod_ready, i * (2 * n) + 2 * n)
                        dve.wait_ge(F.m_placed, i * n + t + 1)
                        dve.tensor_tensor(stage[:, t, :], F.gate[:, 0, t, :], F.gate[:, 1, t, :], ALU.add
                                          ).then_inc(F.mixed, 1)
                    dve.sem_inc(F.mix_read, 2 * n)
                    experts(2, i)
                dve.wait_ge(F.x_again, 16)
                for i in range(NCH):
                    dve.wait_ge(piece_done, F.after(OUT + i))
                    for t in range(n):
                        ht = F.h[:, t, i * CW:(i + 1) * CW]
                        dve.tensor_tensor(ht, ps[:, 2 * (i % 2) + t, :], ht, ALU.add).then_inc(F.h_ready, 1)
                    experts(1)
                dve.wait_ge(F.h_squared, n)
                root(rstd[:, 1, t0:t0 + n], ssq[:, 1, t0:t0 + n], nwork[:, t0:t0 + n], D)
                dve.wait_ge(F.ln2_loaded, 16)
                for t in range(n):
                    dve.scalar_tensor_tensor(F.xn2[:, t, :], F.h[:, t, :], rstd[:, 1, t0 + t:t0 + t + 1], ln2b,
                                             ALU.mult, ALU.mult).then_inc(F.xn2_ready, 1)
                experts(2)
                for i in range(NCH):
                    experts(2)

            def top8(value, index, work_, half):
                both = list(zip(value, index, work_))
                lo = 8 * half
                for v_, _, w in both:
                    step(dve.max(v_[:, lo:lo + 8], w))
                settle()
                for v_, x, w in both:
                    step(dve.max_index(x[:, lo:lo + 8], v_[:, lo:lo + 8], w))
                settle()
                if half == 0:
                    for v_, _, w in both:
                        step(dve.match_replace(w, v_[:, 0:8], w, -3.0e38))
                    settle()

            def pick(F, k, cand_at, onehot_at):
                t = (2, 0, 1)[k]
                cand = cand_at.rearrange("p (h n) -> p h n", h=PH)
                onehot = onehot_at.rearrange("p (s k) -> p s k", k=TOPK)
                best = gates[:, t, :].rearrange("p (h k) -> p h k", h=PH)

                def keys(half, lo, hi):
                    def run():
                        r = range(lo, hi)
                        top8([kval[:, b, :] for b in r], [kidx[:, b, :] for b in r],
                             [F.pkeys[:, t - F.tiles[0], b, :] for b in r], half)
                    return run

                def sums():
                    for h in range(PH):
                        step(dve.tensor_tensor(cand[:, h, :].rearrange("p (i j) -> p i j", i=TOPK),
                                               kval[:, 2 * h, :].unsqueeze(2).to_broadcast([P, TOPK, TOPK]),
                                               kval[:, 2 * h + 1, :].unsqueeze(1).to_broadcast([P, TOPK, TOPK]),
                                               ALU.add))
                    settle()

                def bests(half):
                    def run():
                        r = range(PH)
                        top8([best[:, h, :] for h in r], [cidx[:, h, :] for h in r], [cand[:, h, :] for h in r], half)
                    return run

                def places():
                    link(dve.tensor_copy(bmax[:, :], best[:, :, 0]))
                    dve.tensor_tensor(best, best, bmax[:, :].unsqueeze(2).to_broadcast([P, PH, TOPK]),
                                      ALU.subtract).then_inc(best_ready, 1)
                    flat = cidx[:, :, :].rearrange("p h k -> p (h k)")
                    step(dve.tensor_scalar(cij[:, 0, :], flat, 4, None, ALU.logical_shift_right))
                    step(dve.tensor_scalar(cij[:, 1, :], flat, 15, None, ALU.bitwise_and))
                    step(dve.tensor_copy(kidf[:, :, :], kidx[:, :, :]))
                    settle()
                    link(dve.tensor_copy(cijf[:, :, :], cij[:, :, :]))

                def lookup(half):
                    def run():
                        link(dve.tensor_tensor(onehot, cijf[:, half, :].unsqueeze(2).to_broadcast([P, SLOTS, TOPK]),
                                               iota16[:, :].unsqueeze(1).to_broadcast([P, SLOTS, TOPK]),
                                               ALU.is_equal))
                        k4 = kidf[:, :, :].rearrange("p (h s) k -> p h s k", s=2)[:, :, half, :]
                        o4 = onehot.rearrange("p (h k) i -> p h k i", h=PH)
                        link(dve.tensor_tensor(o4, o4, k4.unsqueeze(2).to_broadcast([P, PH, TOPK, TOPK]), ALU.mult))
                        link(dve.tensor_reduce(cijf[:, half, :], onehot, AX, ALU.add))
                    return run

                def finish():
                    link(dve.scalar_tensor_tensor(cijf[:, 0, :], cijf[:, 0, :], float(P), cijf[:, 1, :], ALU.mult,
                                                  ALU.add))
                    link(dve.tensor_copy(eidx[:, t, :], cijf[:, 0, :]))
                    dve.wait_ge(gate_exp, k + 1)
                    link(dve.tensor_reduce(bsum[:, :], best, AX, ALU.add))
                    link(dve.reciprocal(bsum[:, :], bsum[:, :]))
                    dve.tensor_tensor(best, best, bsum[:, :].unsqueeze(2).to_broadcast([P, PH, TOPK]),
                                      ALU.mult).then_inc(picked, 1)
                    dve.wait_ge(picked, k + 1)

                if F.streams:
                    lists = [keys(half, i * HC, (i + 1) * HC) for i in range(NCH) for half in range(2)]
                else:
                    lists = [keys(half, i * PH, (i + 1) * PH) for half in range(2) for i in range(2)]
                return lists + [sums, bests(0), bests(1),
                        places, lookup(0), lookup(1), finish]

            gflat = gates[:, :, :].rearrange("p t s -> p (t s)")

            def expert_acts(E, tau):
                dve.wait_ge(E.gelu_done, tau)
                dve.wait_ge(E.v_free, tau * TURN + (len(E.vrow) - TURN))
                dve.tensor_tensor(acts[:, :], gelu[:, :], gflat[:, bass.ds(tau * TURN + (E.first - TURN), TURN)],
                                  ALU.mult).then_inc(E.acts_ready, 1)
                dve.wait_ge(E.acts_ready, tau)

            def add_row(E, tau, s, h):
                NV = len(E.vrow)
                dve.wait_ge(E.v_loaded[s], tau * 16)
                dve.wait_ge(E.v_free, tau * TURN + (s - TURN + NV))
                dve.scalar_tensor_tensor(h, E.vrow[s], acts[:, s:s + 1], h, ALU.mult, ALU.add).then_inc(E.v_free, 1)

            def expert_turn(E, tau, xn, h, first=False, slots=range(TURN)):
                NU = len(E.urow)
                if not first and slots[0] == 0:
                    expert_acts(E, tau)
                for s in slots:
                    u, per = s % NU, TURN // NU
                    dve.wait_ge(E.u_loaded[u], tau * (16 * per) + 16 * (s // NU + 1))
                    dve.scalar_tensor_tensor(E.urow[u], E.urow[u], 1.0, xn, ALU.mult, ALU.mult,
                                             accum_out=dots[:, s:s + 1]).then_inc(E.u_free, 1)
                    if not first:
                        add_row(E, tau, s, h)

            def last_rows(E, tau, h):
                expert_acts(E, tau)
                for s in range(TURN):
                    add_row(E, tau, s, h)

            prepare(S)
            front(S, lambda *_: None)
            dve.wait_ge(made, CONSTS)
            for k, stage_ in enumerate(pick(S, 0, xTs_flat, rows[:, 0, :])):
                if k < 2 * NCH and k % 2 == 0:
                    dve.wait_ge(S.key_read, k // 2 + 1)
                stage_()
            dve.sem_inc(ES.u_free, len(ES.urow))
            dve.sem_inc(ES.v_free, len(ES.vrow))

            streams_place = Place()

            def stream_turns(halves, i=None):
                for tau, half in streams_place.next(halves, i):
                    expert_turn(ES, tau, S.xn2[:, 0, :], S.h[:, 0, :], first=streams_place.first(tau),
                                slots=range(half * TURN // 2, (half + 1) * TURN // 2))

            front(R, stream_turns)
            dve.wait_ge(R.key_read, 2 * NCH)
            first, second = xTr_flat[:, 0:D], xTr_flat[:, D:2 * D]
            stages = pick(R, 1, first, second)
            assert TURNS - streams_place.turns == LATE_TURNS
            for k, stage_ in enumerate(stages):
                stage_()
                if k in (1, 3, 5, 6, 8):
                    stream_turns(2)
            dve.sem_inc(ER.u_free, len(ER.urow))
            last_rows(ES, TURNS, S.h[:, 0, :])
            dve.sem_inc(ER.v_free, len(ER.vrow))
            stages = pick(R, 2, first, second)
            assert len(stages) == PEELED - 1
            expert_turn(ER, 0, R.xn2[:, 0, :], R.h[:, 0, :], first=True)
            for tau in range(1, PEELED):
                stages[tau - 1]()
                expert_turn(ER, tau, R.xn2[:, 0, :], R.h[:, 0, :])
            with dve.Fori(PEELED, TURNS) as tau:
                expert_turn(ER, tau, R.xn2[:, 0, :], R.h[:, 0, :])
            expert_acts(ER, TURNS)
            for s in range(TURN):
                dve.wait_ge(ER.u_loaded[s], 16 * (TURNS + 1))
                dve.scalar_tensor_tensor(ER.urow[s], ER.urow[s], 1.0, R.xn2[:, 1, :], ALU.mult, ALU.mult,
                                         accum_out=dots[:, s:s + 1]).then_inc(ER.u_free, 1)
                add_row(ER, TURNS, s, R.h[:, 0, :])
            with dve.Fori(TURNS + 1, 2 * TURNS) as tau:
                expert_turn(ER, tau, R.xn2[:, 1, :], R.h[:, 1, :])
            last_rows(ER, 2 * TURNS, R.h[:, 1, :])


def kernel(x_prompt, x_sample, cache_a_k, cache_a_v, cache_b_k, cache_b_v, cache_b_lf, ln1, w_in, b_f,
           qn_a, kn_a, qn_b, kn_b, rel_bias, w_br_a, w_br_b, w_out, ln2, w_pq, sub_keys, peer_u, peer_v):
    import numpy as np
    import concourse.bacc as bacc
    from concourse.bass_utils import run_bass_kernel_spmd

    def tidy(z):
        return np.ascontiguousarray(z)

    x = np.concatenate([np.asarray(x_prompt)[0], np.asarray(x_sample).reshape(P, D)], axis=0)
    w_in0 = np.asarray(w_in)[0]
    table = np.asarray(rel_bias)[0]
    q, k = np.arange(P)[:, None], np.arange(P)[None, :]

    def spread(distance):
        return tidy(table[:, np.clip(distance, -P, P) + P].transpose(1, 0, 2).reshape(P, HEADS * P))

    def turned(z):
        return tidy(z.T.reshape(KT, P, -1).transpose(1, 0, 2).reshape(P, -1))

    def keys(c):
        return tidy(np.asarray(c)[0].transpose(3, 2, 0, 1).reshape(P, HEADS * STREAMS * P))

    def values(c):
        return tidy(np.asarray(c)[0].transpose(1, 2, 0, 3).reshape(P, HEADS * STREAMS * P))

    ins = {
        "x": x,
        "xTr": turned(x[:2 * P]), "xTs": turned(x[2 * P:]),
        "ln1": tidy(np.asarray(ln1)[0].reshape(KT, P).T),
        "ln2": tidy(np.asarray(ln2)[0]),
        "b_f": tidy(np.asarray(b_f)[0]),
        "w_f": tidy(w_in0[:, FCOL:GCOL].reshape(KT, P, HEADS).transpose(1, 0, 2).reshape(P, KT * HEADS)),
        "w_in": w_in0,
        "clf": tidy(np.asarray(cache_b_lf)[0].transpose(1, 2, 0).reshape(P, HEADS * STREAMS)),
        "subT": tidy(np.asarray(sub_keys)[0].transpose(2, 0, 1).reshape(P, 2 * P)),
        "qn_a": np.asarray(qn_a)[0], "kn_a": np.asarray(kn_a)[0],
        "qn_b": np.asarray(qn_b)[0], "kn_b": np.asarray(kn_b)[0],
        "relD": spread(q - k), "relL": spread(P + q - k), "relC": spread(P + q % SQ - k),
        "ckT_a": keys(cache_a_k), "ckT_b": keys(cache_b_k),
        "cv_a": values(cache_a_v), "cv_b": values(cache_b_v),
        "w_br_a": np.asarray(w_br_a)[0], "w_br_b": np.asarray(w_br_b)[0],
        "w_out": np.asarray(w_out)[0], "w_pq": np.asarray(w_pq)[0],
        "peer_u": np.asarray(peer_u)[0], "peer_v": np.asarray(peer_v)[0],
    }
    outs = {"y": (T, D), "k_a": (T, WIDTH), "v_a": (T, WIDTH), "k_b": (T, WIDTH), "v_b": (T, WIDTH), "lf": (T, HEADS)}
    nc = bacc.Bacc("TRN2", target_bir_lowering=False, num_devices=1)
    arrays, aps = {}, {}
    for name, z in ins.items():
        arrays[f"in_{name}"] = np.ascontiguousarray(z)
        aps[name] = nc.dram_tensor(f"in_{name}", z.shape, F32, kind="ExternalInput").ap()
    for name, shape in outs.items():
        aps[name] = nc.dram_tensor(f"out_{name}", shape, F32, kind="ExternalOutput").ap()
    build(nc, aps)
    r = run_bass_kernel_spmd(nc, [arrays], core_ids=[0]).results[0]
    got = {name: np.asarray(r[f"out_{name}"]) for name in outs}
    S = TT * P - P

    def prompt(z, *rest):
        return z[:S].reshape(1, 1, S, *rest)

    def sample(z, *rest):
        return z[S:].reshape(1, STREAMS, SQ, *rest)

    hd = (HEADS, P)
    return (got["y"][:S].reshape(1, S, D), got["y"][S:].reshape(STREAMS, SQ, D),
            prompt(got["k_a"], *hd), prompt(got["v_a"], *hd), sample(got["k_a"], *hd), sample(got["v_a"], *hd),
            prompt(got["k_b"], *hd), prompt(got["v_b"], *hd), prompt(got["lf"], HEADS),
            sample(got["k_b"], *hd), sample(got["v_b"], *hd), sample(got["lf"], HEADS))
```
